# Optimizing a Trainium2 kernel written in Bass

```python
import jax, jax.numpy as jnp
from jax import lax
import numpy as np

D_MODEL = 1024
BATCH = 1
SEQ = 256
DEPTH = 2
DEC_BATCH = 8
DEC_SEQ = 4
PAST_LEN = 2048
PAGE_SIZE = 128

N_MIXERS = 2
N_A_LAYERS = (DEPTH + 1) // 2
N_B_LAYERS = DEPTH // 2
CHUNK = 128
D_A = 2 * D_MODEL
N_GROUPS_A = 8
D_GROUP_A = D_A // N_GROUPS_A
D_B = D_MODEL
CONV_W = 3
PEER_HEADS = 8
N_KEYS = 128
N_EXPERTS = N_KEYS * N_KEYS
D_QUERY = 256
D_HALF = D_QUERY // 2
TOPK_HALF = 16
TOPK = 16
PEER_BLOCK = 256
EPS = 1e-6

kernel_name = "hybrid_gmlp_shortconv_peer_step"

def rms_norm(x, g):
    xf = x.astype(jnp.float32)
    y = xf * lax.rsqrt(jnp.mean(xf * xf, axis=-1, keepdims=True) + EPS)
    return (y * g.astype(jnp.float32)).astype(x.dtype)

def layer_norm(x, g, b):
    xf = x.astype(jnp.float32)
    mu = jnp.mean(xf, axis=-1, keepdims=True)
    var = jnp.mean(jnp.square(xf - mu), axis=-1, keepdims=True)
    y = (xf - mu) * lax.rsqrt(var + EPS)
    return (y * g.astype(jnp.float32) + b.astype(jnp.float32)).astype(x.dtype)

def chunk_mlp_mixer(x, w_in, ln_g, ln_b, w_s, b_s, w_out):
    bsz, s_len, _ = x.shape
    L = min(s_len, CHUNK)
    C = s_len // L
    z = jax.nn.gelu(x @ w_in)
    u, v = jnp.split(z, 2, axis=-1)
    v = layer_norm(v, ln_g, ln_b)
    mask = jnp.tril(jnp.ones((L, L), dtype=bool))
    ws = jnp.where(mask[None], w_s[:, :L, :L], 0).astype(v.dtype)
    vc = v.reshape(bsz, C, L, N_GROUPS_A, D_GROUP_A)
    bias = jnp.transpose(b_s[:, :L]).astype(v.dtype)
    mixed = jnp.einsum('gij,bcjgd->bcigd', ws, vc) + bias[None, None, :, :, None]
    y = (u * mixed.reshape(bsz, s_len, D_A)) @ w_out
    return y, v

def short_conv_mixer(x, buf, w_in, conv_w, w_out):
    s_len = x.shape[1]
    b_gate, c_gate, h = jnp.split(x @ w_in, 3, axis=-1)
    z = c_gate * h
    zp = jnp.concatenate([buf.astype(z.dtype), z], axis=1)
    conv = sum(conv_w[k] * zp[:, k:k + s_len] for k in range(CONV_W))
    y = (b_gate * conv) @ w_out
    return y, zp[:, s_len:]

def peer_ffn(h, w_query, sub_keys, expert_u, expert_v):
    n_tok = h.shape[0]
    n_blk = -(-n_tok // PEER_BLOCK)
    hp = jnp.pad(h, ((0, n_blk * PEER_BLOCK - n_tok), (0, 0))).reshape(n_blk, PEER_BLOCK, D_MODEL)

    def block(xb):
        q = (xb @ w_query).reshape(PEER_BLOCK, PEER_HEADS, 2, D_HALF)
        s = jnp.einsum('thpd,hpkd->thpk', q.astype(jnp.float32), sub_keys.astype(jnp.float32))
        sv, si = lax.top_k(s, TOPK_HALF)
        cand = sv[:, :, 0, :, None] + sv[:, :, 1, None, :]
        cv, ci = lax.top_k(cand.reshape(PEER_BLOCK, PEER_HEADS, TOPK_HALF * TOPK_HALF), TOPK)
        i1 = jnp.take_along_axis(si[:, :, 0], ci // TOPK_HALF, axis=-1)
        i2 = jnp.take_along_axis(si[:, :, 1], ci % TOPK_HALF, axis=-1)
        idx = i1 * N_KEYS + i2
        g = jax.nn.softmax(cv, axis=-1)
        u_sel = expert_u[idx]
        a = jax.nn.gelu(jnp.einsum('thkd,td->thk', u_sel, xb))
        return jnp.einsum('thk,thkd->td', g.astype(a.dtype) * a, expert_v[idx])

    out = lax.map(block, hp)
    return out.reshape(n_blk * PEER_BLOCK, D_MODEL)[:n_tok]

def setup_inputs(seed: int = 0) -> dict:
    key = jax.random.key(seed)
    ks = jax.random.split(key, 20)
    f32 = jnp.float32
    nrm = lambda k, shape, scale: jax.random.normal(k, shape, f32) * scale
    return {
        "x_prompt": nrm(ks[0], (BATCH, SEQ, D_MODEL), 1.0),
        "x_sample": nrm(ks[1], (DEC_BATCH, DEC_SEQ, D_MODEL), 1.0),
        "state_conv": nrm(ks[2], (N_B_LAYERS, DEC_BATCH, CONV_W - 1, D_B), 0.5),
        "norm_mix": 1.0 + nrm(ks[3], (DEPTH, D_MODEL), 0.02),
        "norm_ffn": 1.0 + nrm(ks[4], (DEPTH, D_MODEL), 0.02),
        "norm_final": 1.0 + nrm(ks[5], (D_MODEL,), 0.02),
        "a_w_in": nrm(ks[6], (N_A_LAYERS, D_MODEL, 2 * D_A), D_MODEL ** -0.5),
        "a_ln_g": 1.0 + nrm(ks[7], (N_A_LAYERS, D_A), 0.02),
        "a_ln_b": nrm(ks[8], (N_A_LAYERS, D_A), 0.02),
        "a_w_s": nrm(ks[9], (N_A_LAYERS, N_GROUPS_A, CHUNK, CHUNK), CHUNK ** -0.5),
        "a_b_s": 1.0 + nrm(ks[10], (N_A_LAYERS, N_GROUPS_A, CHUNK), 0.02),
        "a_w_out": nrm(ks[11], (N_A_LAYERS, D_A, D_MODEL), D_A ** -0.5),
        "b_w_in": nrm(ks[12], (N_B_LAYERS, D_MODEL, 3 * D_B), D_MODEL ** -0.5),
        "b_conv_w": nrm(ks[13], (N_B_LAYERS, CONV_W, D_B), CONV_W ** -0.5),
        "b_w_out": nrm(ks[14], (N_B_LAYERS, D_B, D_MODEL), D_B ** -0.5),
        "peer_w_query": nrm(ks[15], (DEPTH, D_MODEL, PEER_HEADS * D_QUERY), D_MODEL ** -0.5),
        "peer_sub_keys": nrm(ks[16], (DEPTH, PEER_HEADS, 2, N_KEYS, D_HALF), D_HALF ** -0.5),
        "peer_expert_u": nrm(ks[17], (DEPTH, N_EXPERTS, D_MODEL), D_MODEL ** -0.5),
        "peer_expert_v": nrm(ks[18], (DEPTH, N_EXPERTS, D_MODEL), 0.5 * PEER_HEADS ** -0.5),
    }

def reference(x_prompt, x_sample, state_conv, norm_mix, norm_ffn, norm_final,
              a_w_in, a_ln_g, a_ln_b, a_w_s, a_b_s, a_w_out,
              b_w_in, b_conv_w, b_w_out,
              peer_w_query, peer_sub_keys, peer_expert_u, peer_expert_v):
    xp, xs = x_prompt, x_sample
    n_prompt_tok = BATCH * SEQ
    v_rows_sample, conv_prompt, conv_sample = [], [], []
    for i in range(DEPTH):
        j = i // N_MIXERS
        hp = rms_norm(xp, norm_mix[i])
        hs = rms_norm(xs, norm_mix[i])
        if i % N_MIXERS == 0:
            yp, _ = chunk_mlp_mixer(hp, a_w_in[j], a_ln_g[j], a_ln_b[j], a_w_s[j], a_b_s[j], a_w_out[j])
            ys, vs = chunk_mlp_mixer(hs, a_w_in[j], a_ln_g[j], a_ln_b[j], a_w_s[j], a_b_s[j], a_w_out[j])
            v_rows_sample.append(vs)
        else:
            zero_buf = jnp.zeros((BATCH, CONV_W - 1, D_B), hp.dtype)
            yp, bp = short_conv_mixer(hp, zero_buf, b_w_in[j], b_conv_w[j], b_w_out[j])
            ys, bs = short_conv_mixer(hs, state_conv[j], b_w_in[j], b_conv_w[j], b_w_out[j])
            conv_prompt.append(bp)
            conv_sample.append(bs)
        xp = xp + yp
        xs = xs + ys
        tok = jnp.concatenate([rms_norm(xp, norm_ffn[i]).reshape(-1, D_MODEL),
                               rms_norm(xs, norm_ffn[i]).reshape(-1, D_MODEL)], axis=0)
        f = peer_ffn(tok, peer_w_query[i], peer_sub_keys[i], peer_expert_u[i], peer_expert_v[i])
        xp = xp + f[:n_prompt_tok].reshape(xp.shape)
        xs = xs + f[n_prompt_tok:].reshape(xs.shape)
    y_prompt = rms_norm(xp, norm_final)
    y_sample = rms_norm(xs, norm_final)
    return (y_prompt, y_sample, jnp.stack(v_rows_sample), jnp.stack(conv_prompt), jnp.stack(conv_sample))


_drawn_inputs = setup_inputs


def setup_inputs(seed=0):
    import zlib

    import numpy as np

    out = dict(_drawn_inputs(seed))
    spreads = {}
    factors = {'norm_ffn': 3.031, 'norm_final': 7.282, 'a_ln_g': 2.82, 'a_ln_b': 4.316}
    for name, (base, spread) in spreads.items():
        noise = np.random.default_rng([zlib.crc32(name.encode()), seed]).standard_normal(out[name].shape)
        drawn = base * np.exp(spread * noise) if base else spread * noise
        out[name] = __import__('jax').numpy.asarray(drawn.astype(out[name].dtype))
    for name, factor in factors.items():
        out[name] = (out[name] * factor).astype(out[name].dtype)
    return out
```

```python
from contextlib import ExitStack

import numpy as np

import concourse.bass as bass
from concourse import mybir

F32 = mybir.dt.float32
U32 = mybir.dt.uint32
ALU = mybir.AluOpType
ACT = mybir.ActivationFunctionType
AX_X = mybir.AxisListType.X

P = 128
D = 1024
KD = D // P
DA = 2 * D
LAYERS = 2
NT = 3
ROWS = [128, 128, 32]
COL = [0, 128, 256]
TOK = 288
SB, SS = 8, 4
HEADS, NKEYS, TOPK = 8, 128, 16
HP = 2 * HEADS
EXPERTS = NKEYS * NKEYS
GROUPS = 8
EPS = 1e-6
WCOLS = 512
RING = 8
FOLD = P // 32
HEADS_OF = [HEADS, HEADS, HEADS // FOLD]
HEAD0 = [0, HEADS_OF[0], HEADS_OF[0] + HEADS_OF[1]]
LAYER_HEADS = sum(HEADS_OF)
NEG = -3.0e38
ROOTS_MIX, ROOTS_LN, ROOTS_FFN, ROOTS_FINAL = [0, 9], 3, [6, 12], 15

CHUNKS = (
    [("a_in", DA + c * WCOLS, 0) for c in range(4)] + [("a_in", c * WCOLS, 0) for c in range(4)]
    + [("a_out", n * WCOLS, h * D) for n in range(2) for h in range(2)]
    + [("wq0", c * WCOLS, 0) for c in range(4)]
    + [("b_in", m * D + c * WCOLS, 0) for m, c in ((1, 0), (2, 0), (1, 1), (2, 1), (0, 0), (0, 1))]
    + [("b_out", n * WCOLS, 0) for n in range(2)]
    + [("wq1", c * WCOLS, 0) for c in range(4)]
)


def plan_groups():
    order = []
    for l in range(LAYERS):
        order += [("xT", l, 0, t, j) for t in range(NT) for j in range(2)]
        if l == 0:
            order += [("v", c, t) for c in range(4) for t in range(NT)]
            order += [("u", b) for b in range(16)]
            order += [("mix", b) for b in range(16)]
        else:
            order += [("bch", n, j) for n in range(6) for j in range(4)]
        order += [("out", l, n, t) for n in range(2) for t in range(NT)]
        order += [("xT", l, 1, t, j) for t in range(NT) for j in range(2)]
        order += [("q", l, b) for b in range(HP)]
        order += [("s", l, t, j) for t in range(NT) for j in range(4)]
        order += [("fold", l, n) for n in range(2)]

    def reader(key):
        if key[0] in ("mix", "out", "fold") or (key[0] == "bch" and key[1] not in (0, 2)):
            return "vector"
        return "scores" if key[0] == "s" else "scalar"

    groups, bank, ranks, last = {}, 0, {"vector": 0, "scalar": 0, "scores": 0}, {}
    for i, key in enumerate(order):
        if key[0] == "s" and key[3] == 0:
            bank = -(-bank // 4) * 4
        who = reader(key)
        rank = ranks[who] = ranks[who] + 1
        b = bank % 8
        groups[key] = (i, b, who, rank, last.get(b))
        last[b] = (who, rank, key)
        bank += 1
    return groups


def trunk(nc, x_tok, w_chunks, gains, ln_gain, ln_bias, w_s, b_s, conv_w, conv_state, sub_keys,
          expert_u, expert_v, ident_c, iota_c, fold_c, tril_c, smask_c,
          y_tok, v_rows, conv_prompt, conv_sample):
    G = plan_groups()
    with ExitStack() as ctx:
        def sb(name, shape, dt=F32):
            return ctx.enter_context(nc.sbuf_tensor(name, shape, dt))

        def sem(name):
            return ctx.enter_context(nc.semaphore(name))

        x = [sb(f"x{t}", [P, D]) for t in range(NT)]
        xn = [sb(f"xn{t}", [P, D]) for t in range(NT)]
        acc2 = sb("acc2", [P, D])
        xT = sb("xT", [P, KD, TOK])
        wring = sb("wring", [P, 2, KD, WCOLS])
        arena = sb("arena", [P, 2 * RING * D])
        qT = sb("qT", [P, HP, TOK])
        keys = sb("keys", [P, HP, NKEYS])
        gain = sb("gain", [P, 2, D])
        ws = sb("ws", [P, GROUPS, P])
        wsm = sb("wsm", [P, GROUPS, P])
        ws2 = sb("ws2", [32, GROUPS, SS])
        wsm2 = sb("wsm2", [32, GROUPS, SB, SS])
        brow = sb("brow", [1, GROUPS, P])
        ident = sb("ident", [P, P])
        ones = sb("ones", [1, P])
        iota = sb("iota", [P, TOPK])
        fold = sb("fold", [P, 32])
        tril = sb("tril", [P, P], U32)
        smask = sb("smask", [32, SB, SS], U32)
        convw = sb("convw", [P, 3, KD])
        state = sb("state", [P, KD, SB, 2])
        cpn = sb("cpn", [P, KD, 2])
        csn = sb("csn", [P, KD, SB, 2])
        stats = sb("stats", [P, NT, 4, 6])
        mv = sb("mv", [P, NT, 2])
        root = sb("root", [P, NT])
        rstd = sb("rstd", [P, NT])
        msq = sb("msq", [P, NT])
        idx = sb("idx", [P, NT, HEADS * TOPK], U32)
        gate = sb("gate", [P, NT, HEADS * TOPK])
        idx2 = sb("idx2", [P, HEADS_OF[2] * TOPK], U32)
        gate2 = sb("gate2", [P, HEADS_OF[2] * TOPK])
        stage = sb("stage", [P, 2, 2, RING], U32)
        a_raw = sb("a_raw", [P, TOPK])
        a_gelu = sb("a_gelu", [P, TOPK])
        wgt = sb("wgt", [P, TOPK])
        sh = sb("sh", [P, 2, NKEYS])
        tv = sb("tv", [P, 2, TOPK])
        ti = sb("ti", [P, 2, TOPK], U32)
        tif = sb("tif", [P, 2, TOPK])
        cand = sb("cand", [P, TOPK, TOPK])
        cv = sb("cv", [P, TOPK])
        ci = sb("ci", [P, TOPK], U32)
        cpos = sb("cpos", [P, 2, TOPK], U32)
        cposf = sb("cposf", [P, 2, TOPK])
        pick = sb("pick", [P, 2, TOPK, TOPK])
        picked = sb("picked", [P, 2, TOPK])
        eidx = sb("eidx", [P, TOPK])
        shifted = sb("shifted", [P, TOPK])
        eexp = sb("eexp", [P, TOPK])
        esum = sb("esum", [P, 1])
        erec = sb("erec", [P, 1])

        o = 16 * TOK
        uT = arena[:, 0:o].rearrange("p (b t) -> p b t", t=TOK)
        v = [arena[:, o + t * DA:o + (t + 1) * DA] for t in range(NT)]
        o += NT * DA
        lng, lnb = arena[:, o:o + DA], arena[:, o + DA:o + 2 * DA]
        assert o + 2 * DA <= 2 * RING * D
        o = KD * TOK
        cT = arena[:, 0:o].rearrange("p (k t) -> p k t", t=TOK)
        gT = arena[:, o:2 * o].rearrange("p (k t) -> p k t", t=TOK)
        zP = arena[:, 2 * o:2 * o + KD * 258].rearrange("p (k t) -> p k t", t=258)
        o = 2 * o + KD * 258
        zS = arena[:, o:o + KD * SB * 6].rearrange("p (k b s) -> p k b s", b=SB, s=6)
        uring = arena[:, 0:RING * D].rearrange("p (r d) -> p r d", d=D)
        vring = arena[:, RING * D:2 * RING * D].rearrange("p (r d) -> p r d", d=D)

        psum = ctx.enter_context(nc.psum_tensor("psum", [P, 8 * 512], F32))

        def bank(key, n=512, rows=P, at=0):
            b = G[key][1]
            return psum[0:rows, b * 512 + at:b * 512 + at + n]

        x_landed, const_landed = sem("x_landed"), sem("const_landed")
        gain_landed, keys_landed = sem("gain_landed"), sem("keys_landed")
        w_landed = [sem(f"w_landed{r}") for r in range(2)]
        w_used = sem("w_used")
        group_done = sem("group_done")
        vector_read, scalar_read, scores_copied = sem("vector_read"), sem("scalar_read"), sem("scores_copied")
        step = sem("step")
        xn_ready = sem("xn_ready")
        root_asked, root_taken = sem("root_asked"), sem("root_taken")
        v_normed, ws_ready, gated = sem("v_normed"), sem("ws_ready"), sem("gated")
        route_started, exp_ready, exp_done, routed = (
            sem("route_started"), sem("exp_ready"), sem("exp_done"), sem("routed"))
        xn2_spread, idx2_ready = sem("xn2_spread"), sem("idx2_ready")
        ws2_landed = sem("ws2_landed")
        staged, granted = sem("staged"), sem("granted")
        granted_act, granted_dve = sem("granted_act"), sem("granted_dve")
        u_landed = [sem(f"u_landed{r}") for r in range(RING)]
        v_landed = [sem(f"v_landed{r}") for r in range(RING)]
        u_used, v_used = sem("u_used"), sem("v_used")
        gelu_done, w_ready = sem("gelu_done"), sem("w_ready")
        y_ready, conv_ready = sem("y_ready"), sem("conv_ready")
        v_rows_out, conv_out, y_out = sem("v_rows_out"), sem("conv_out"), sem("y_out")

        N_CONST = 11
        block = ctx.enter_context(nc.Block())

        def route_index(l, t):
            return (l * NT + t) * HEADS

        def head_index(l, t):
            return l * LAYER_HEADS + HEAD0[t]

        def wait_group(e, key):
            e.wait_ge(group_done, G[key][0] + 1)

        @block.sync
        def _(sp):
            for t in range(NT):
                sp.dma_start(x[t][0:ROWS[t], :], x_tok[COL[t]:COL[t] + ROWS[t], :]).then_inc(x_landed, 16)
            sp.dma_start(gain[:, 0, :], gains[0:1, :].partition_broadcast(P)).then_inc(gain_landed, 16)
            for dst, src in (
                (ident[:, :], ident_c), (iota[:, :], iota_c), (fold[:, :], fold_c),
                (tril[:, :], tril_c), (smask[:, :, :], smask_c),
                (ws[:, :, :], w_s), (brow[:, :, :], b_s),
            ):
                sp.dma_start(dst, src).then_inc(const_landed, 16)
            for r in range(2):
                sp.dma_start(wring[:, r, :, :], w_chunks[r]).then_inc(w_landed[r], 16)
            sp.dma_start(lng, ln_gain.partition_broadcast(P)).then_inc(const_landed, 16)
            sp.dma_start(lnb, ln_bias.partition_broadcast(P)).then_inc(const_landed, 16)
            with sp.Fori(1, len(CHUNKS) // 2) as i:
                for r in range(2):
                    sp.wait_ge(w_used, 2 * i + r - 1)
                    sp.dma_start(wring[:, r, :, :], w_chunks[2 * i + r]).then_inc(w_landed[r], 16)
            for t in range(NT):
                sp.wait_ge(y_ready, t + 1)
                sp.dma_start(y_tok[COL[t]:COL[t] + ROWS[t], :], xn[t][0:ROWS[t], :]).then_inc(y_out, 16)
            sp.wait_ge(y_out, 16 * NT)

        @block.gpsimd
        def _(pool):
            def half(l, t, hf, i, u, vv):
                H, g0 = HEADS_OF[t], head_index(l, t)
                source = idx2[:, :] if t == 2 else idx[:, t, :]
                if u:
                    nc.gpsimd.tensor_copy(stage[:, hf, 0, :], source[:, bass.ds(i * TOPK + hf * RING, RING)]
                                          ).then_inc(staged, 1)
                if vv:
                    nc.gpsimd.tensor_copy(stage[:, hf, 1, :], source[:, bass.ds((i - 1) * TOPK + hf * RING, RING)]
                                          ).then_inc(staged, 1)
                if u and not vv:
                    count = 1 + hf
                elif u:
                    count = 4 + (i - 1) * 4 + hf * 2
                else:
                    count = 2 + (H - 1) * 4 + hf + 1
                pool.wait_ge(staged, 4 * g0 + count)
                pool.sem_inc(granted, 1)
                for k in range(RING):
                    n = (g0 + i) * TOPK + hf * RING + k
                    if u:
                        if not (isinstance(n, int) and n < RING):
                            pool.wait_ge(u_used, n - RING + 1)
                            pool.sem_inc(granted, 1)
                        pool.indirect_dma_start(
                            uring[:, k, :], None, expert_u,
                            bass.IndirectOffsetOnAxis(ap=stage[:, hf, 0, k:k + 1], axis=0),
                        ).then_inc(u_landed[k], 16)
                    if vv:
                        n = n - TOPK
                        if not (isinstance(n, int) and n < RING):
                            pool.wait_ge(v_used, n - RING + 1)
                            pool.sem_inc(granted, 1)
                        pool.indirect_dma_start(
                            vring[:, k, :], None, expert_v,
                            bass.IndirectOffsetOnAxis(ap=stage[:, hf, 1, k:k + 1], axis=0),
                        ).then_inc(v_landed[k], 16)

            for l in range(LAYERS):
                for t in range(NT):
                    if t < 2:
                        pool.wait_ge(routed, route_index(l, t) + HEADS)
                    else:
                        pool.wait_ge(idx2_ready, l + 1)
                    if l == 0 and t == 0:
                        pool.wait_ge(v_rows_out, 16)
                    H = HEADS_OF[t]
                    for hf in range(2):
                        half(l, t, hf, 0, True, False)
                    for hf in range(2):
                        half(l, t, hf, 1, True, True)
                    if H > 2:
                        with pool.Fori(2, H) as i:
                            for hf in range(2):
                                half(l, t, hf, i, True, True)
                    for hf in range(2):
                        half(l, t, hf, H, False, True)

        @block.tensor
        def _(pe):
            def open_group(key):
                last = G[key][4]
                if last is None:
                    return
                who, rank, k = last
                if who == "scores":
                    pe.wait_ge(scores_copied, route_index(k[1], k[2]) + 2 * k[3] + 2)
                else:
                    pe.wait_ge(vector_read if who == "vector" else scalar_read, rank)

            def transposes(l, which):
                for t in range(NT):
                    pe.wait_ge(xn_ready, (2 * l + which) * NT + t + 1)
                    for j in range(2):
                        key = ("xT", l, which, t, j)
                        open_group(key)
                        r = ROWS[t]
                        for m in range(4):
                            c = (4 * j + m) * P
                            last = nc.tensor.transpose(bank(key, r, at=m * P), xn[t][0:r, c:c + P],
                                                       ident[0:r, 0:r])
                        last.then_inc(group_done, 1)

            def chunk(n):
                pe.wait_ge(w_landed[n % 2], 16 * (n // 2 + 1))
                return wring[:, n % 2, :, :]

            def blocks(n, key_of):
                w = chunk(n)
                for j in range(4):
                    key = key_of(j)
                    open_group(key)
                    for k in range(KD):
                        last = nc.tensor.matmul(bank(key, TOK), w[:, k, j * P:(j + 1) * P], xT[:, k, :],
                                                start=(k == 0), stop=(k == KD - 1))
                    last.then_inc(group_done, 1)
                last_of_chunk()

            def last_of_chunk():
                pe.wait_ge(group_done, self_groups[0])
                pe.sem_inc(w_used, 1)

            self_groups = [0]

            def out_projection(l, n0, act, kblocks):
                per = kblocks // KD
                for n in range(2):
                    for h in range(per):
                        w = chunk(n0 + n * per + h)
                        for t in range(NT):
                            key = ("out", l, n, t)
                            if h == 0:
                                open_group(key)
                            for k in range(KD):
                                kk = h * KD + k
                                mm = nc.tensor.matmul(bank(key, WCOLS, ROWS[t]),
                                                      act[:, kk, COL[t]:COL[t] + ROWS[t]], w[:, k, :],
                                                      start=(kk == 0), stop=(kk == kblocks - 1))
                            if h == per - 1:
                                mm.then_inc(group_done, 1)
                            elif t == NT - 1:
                                mm.then_inc(w_used, 1)
                        if h == per - 1:
                            self_groups[0] = G[("out", l, n, NT - 1)][0] + 1
                            last_of_chunk()

            n0 = 0
            pe.wait_ge(const_landed, 16 * N_CONST)
            for l in range(LAYERS):
                transposes(l, 0)
                pe.wait_ge(scalar_read, G[("xT", l, 0, NT - 1, 1)][3])
                if l == 0:
                    for c in range(4):
                        w = chunk(n0 + c)
                        for t in range(NT):
                            key = ("v", c, t)
                            open_group(key)
                            for k in range(KD):
                                mm = nc.tensor.matmul(bank(key, WCOLS, ROWS[t]),
                                                      xT[:, k, COL[t]:COL[t] + ROWS[t]], w[:, k, :],
                                                      start=(k == 0), stop=(k == KD - 1))
                            mm.then_inc(group_done, 1)
                        self_groups[0] = G[("v", c, NT - 1)][0] + 1
                        last_of_chunk()
                    n0 += 4
                    for c in range(4):
                        self_groups[0] = G[("u", 4 * c + 3)][0] + 1
                        blocks(n0 + c, lambda j, c=c: ("u", 4 * c + j))
                    n0 += 4
                    pe.wait_ge(ws_ready, 1)
                    pe.wait_ge(v_normed, NT)
                    for b in range(16):
                        key, g = ("mix", b), b // 2
                        open_group(key)
                        for t in range(NT):
                            r = ROWS[t]
                            out = bank(key, r, at=COL[t])
                            m = wsm[:, g, :] if t < 2 else wsm2[:, g, :, :]
                            bias = (brow[0:1, g, :] if t < 2
                                    else brow[0:1, g:g + 1, 0:SS].to_broadcast([1, SB, SS]))
                            nc.tensor.matmul(out, v[t][0:r, b * P:(b + 1) * P], m, start=True, stop=False)
                            mm = nc.tensor.matmul(out, ones[0:1, :], bias, start=False, stop=True)
                        mm.then_inc(group_done, 1)
                    pe.wait_ge(gated, 16)
                    out_projection(l, n0, uT, 2 * KD)
                    n0 += 4
                else:
                    for c in range(6):
                        self_groups[0] = G[("bch", c, 3)][0] + 1
                        blocks(n0 + c, lambda j, c=c: ("bch", c, j))
                    n0 += 6
                    pe.wait_ge(gated, 16 + KD)
                    out_projection(l, n0, gT, KD)
                    n0 += 2
                transposes(l, 1)
                pe.wait_ge(scalar_read, G[("xT", l, 1, NT - 1, 1)][3])
                for c in range(4):
                    self_groups[0] = G[("q", l, 4 * c + 3)][0] + 1
                    blocks(n0 + c, lambda j, c=c: ("q", l, 4 * c + j))
                n0 += 4
                pe.wait_ge(keys_landed, 16 * (l + 1))
                pe.wait_ge(scalar_read, G[("q", l, HP - 1)][3])
                for t in range(NT):
                    for j in range(4):
                        key = ("s", l, t, j)
                        open_group(key)
                        for m in range(4):
                            hp = 4 * j + m
                            mm = nc.tensor.matmul(bank(key, NKEYS, ROWS[t], at=m * NKEYS),
                                                  qT[:, hp, COL[t]:COL[t] + ROWS[t]], keys[:, hp, :],
                                                  start=True, stop=True)
                        mm.then_inc(group_done, 1)
                pe.wait_ge(v_used, TOPK * (l + 1) * LAYER_HEADS)
                for n in range(2):
                    key = ("fold", l, n)
                    open_group(key)
                    nc.tensor.matmul(bank(key, WCOLS, 32), fold[:, :], acc2[:, n * WCOLS:(n + 1) * WCOLS],
                                     start=True, stop=True).then_inc(group_done, 1)

        @block.scalar
        def _(act):
            act.dma_start(gain[:, 1, :], gains[1:2, :].partition_broadcast(P)).then_inc(gain_landed, 16)
            act.dma_start(keys[:, :, :], sub_keys[0]).then_inc(keys_landed, 16)
            act.dma_start(convw[:, :, :], conv_w).then_inc(const_landed, 16)
            act.dma_start(state[:, :, :, :], conv_state).then_inc(const_landed, 16)
            for b in range(SB):
                act.dma_start(ws2[SS * b:SS * b + SS, :, :], w_s[0:SS, :, 0:SS]).then_inc(ws2_landed, 16)

            def read(key, out, func, n=512, rows=P, shape=None):
                wait_group(act, key)
                src = bank(key, n, rows)
                if shape:
                    src = src.rearrange("p (a b) -> p a b", b=shape)
                nc.scalar.activation(out, src, func).then_inc(scalar_read, 1)

            def roots(first):
                for t in range(NT):
                    act.wait_ge(root_asked, first + t + 1)
                    nc.scalar.activation(root[0:ROWS[t], t:t + 1], root[0:ROWS[t], t:t + 1], ACT.Sqrt
                                         ).then_inc(root_taken, 1)

            def read_transposes(l, which):
                for t in range(NT):
                    for j in range(2):
                        key = ("xT", l, which, t, j)
                        wait_group(act, key)
                        src = bank(key).rearrange("p (a b) -> p a b", b=P)[:, :, 0:ROWS[t]]
                        nc.scalar.copy(xT[:, 4 * j:4 * j + 4, COL[t]:COL[t] + ROWS[t]], src
                                       ).then_inc(scalar_read, 1)

            def route_head(l, t, i):
                r, rows = route_index(l, t), ROWS[t]
                b0 = G[("s", l, t, 0)][1] * 512
                if not (isinstance(i, int) and r + i == 0):
                    act.wait_ge(route_started, r + i)
                    act.sem_inc(granted_act, 1)
                nc.scalar.copy(sh[0:rows, :, :].rearrange("p a b -> p (a b)"),
                               psum[0:rows, bass.ds(b0 + i * 2 * NKEYS, 2 * NKEYS)]).then_inc(scores_copied, 1)
                act.wait_ge(exp_ready, r + i + 1)
                act.sem_inc(granted_act, 1)
                nc.scalar.activation(eexp[0:rows, :], shifted[0:rows, :], ACT.Exp,
                                     accum_out=esum[0:rows, :]).then_inc(exp_done, 1)

            def gelu_head(l, t, i):
                g = head_index(l, t) + i
                if not (isinstance(g, int) and g == 0):
                    act.wait_ge(w_ready, g)
                    act.sem_inc(granted_act, 1)
                act.wait_ge(u_used, TOPK * (g + 1))
                act.sem_inc(granted_act, 1)
                nc.scalar.activation(a_gelu[:, :], a_raw[:, :], ACT.Gelu_apprx_tanh).then_inc(gelu_done, 1)

            for l in range(LAYERS):
                roots(ROOTS_MIX[l])
                read_transposes(l, 0)
                act.dma_start(gain[:, 0, :], gains[2 * (l + 1):2 * (l + 1) + 1, :].partition_broadcast(P)
                              ).then_inc(gain_landed, 16)
                if l == 0:
                    act.wait_ge(const_landed, 16 * N_CONST)
                    for c in range(4):
                        for t in range(NT):
                            read(("v", c, t), v[t][0:ROWS[t], c * WCOLS:(c + 1) * WCOLS], ACT.Gelu_apprx_tanh,
                                 rows=ROWS[t])
                    roots(ROOTS_LN)
                    for b in range(16):
                        read(("u", b), uT[:, b, :], ACT.Gelu_apprx_tanh, n=TOK)
                    act.wait_ge(v_normed, NT)
                    act.dma_start(v_rows, v[2][0:32, :]).then_inc(v_rows_out, 16)
                else:
                    for c in (0, 2):
                        for j in range(4):
                            read(("bch", c, j), cT[:, 2 * c + j, :], ACT.Copy, n=TOK)
                roots(ROOTS_FFN[l])
                read_transposes(l, 1)
                if l == 0:
                    act.dma_start(gain[:, 1, :], gains[3:4, :].partition_broadcast(P)).then_inc(gain_landed, 16)
                for f in range(1, FOLD):
                    nc.scalar.copy(xn[2][32 * f:32 * f + 32, :], xn[2][0:32, :]).then_inc(xn2_spread, 1)
                for b in range(HP):
                    read(("q", l, b), qT[:, b, :], ACT.Copy, n=TOK)
                if l == 1:
                    act.wait_ge(conv_ready, 1)
                    act.dma_start(conv_prompt, cpn[:, :, :]).then_inc(conv_out, 16)
                    act.dma_start(conv_sample, csn[:, :, :, :]).then_inc(conv_out, 16)
                wait_group(act, ("s", l, 0, 3))
                with act.Fori(0, HEADS) as i:
                    route_head(l, 0, i)
                for t in range(NT):
                    if t < 2:
                        wait_group(act, ("s", l, t + 1, 3))
                        if l == 0 and t == 1:
                            act.dma_start(keys[:, :, :], sub_keys[1]).then_inc(keys_landed, 16)
                        with act.Fori(0, HEADS) as i:
                            route_head(l, t + 1, i)
                            gelu_head(l, t, i)
                    else:
                        for i in range(HEADS_OF[t]):
                            gelu_head(l, t, i)
            roots(ROOTS_FINAL)
            act.wait_ge(v_rows_out, 16)
            act.wait_ge(conv_out, 32)

        @block.vector
        def _(dve):
            steps = [0]

            def did(instruction):
                steps[0] += 1
                instruction.then_inc(step, 1)
                return steps[0]

            def after(n):
                dve.wait_ge(step, n)

            def reciprocal_roots(first):
                n = steps[0]
                after(n)
                for t in range(NT):
                    r = ROWS[t]
                    nc.vector.tensor_scalar(root[0:r, t:t + 1], msq[0:r, t:t + 1], EPS, None, ALU.add
                                            ).then_inc(root_asked, 1)
                for t in range(NT):
                    r = ROWS[t]
                    dve.wait_ge(root_taken, first + t + 1)
                    n = did(nc.vector.reciprocal(rstd[0:r, t:t + 1], root[0:r, t:t + 1]))
                after(n)

            def norm(which, first, sem_done):
                for t in range(NT):
                    r = ROWS[t]
                    did(nc.vector.scalar_tensor_tensor(
                        out=xn[t][0:r, :], in0=x[t][0:r, :], scalar=1.0 / D, in1=x[t][0:r, :],
                        op0=ALU.mult, op1=ALU.mult, accum_out=msq[0:r, t:t + 1]))
                reciprocal_roots(first)
                for t in range(NT):
                    r = ROWS[t]
                    nc.vector.scalar_tensor_tensor(
                        out=xn[t][0:r, :], in0=x[t][0:r, :], scalar=rstd[0:r, t:t + 1],
                        in1=gain[0:r, which, :], op0=ALU.mult, op1=ALU.mult).then_inc(sem_done, 1)

            def add_group(key, t):
                c = key[2] * WCOLS
                wait_group(dve, key)
                r = ROWS[t]
                nc.vector.tensor_tensor(x[t][0:r, c:c + WCOLS], x[t][0:r, c:c + WCOLS],
                                        bank(key, WCOLS, r), ALU.add).then_inc(vector_read, 1)

            def route(l, t, i):
                R = ROWS[t]
                r = route_index(l, t) + i
                V = nc.vector

                def top16(values, best, where):
                    V.max(best[:, 0:8], values)
                    dve.drain()
                    V.max_index(where[:, 0:8], best[:, 0:8], values)
                    dve.drain()
                    V.match_replace(values, best[:, 0:8], values, NEG)
                    dve.drain()
                    V.max(best[:, 8:16], values)
                    dve.drain()
                    V.max_index(where[:, 8:16], best[:, 8:16], values)

                def halves():
                    dve.wait_ge(scores_copied, r + 1)
                    dve.sem_inc(granted_dve, 1)
                    dve.drain()
                    for op in range(5):
                        for p in range(2):
                            s, b, w = sh[0:R, p, :], tv[0:R, p, :], ti[0:R, p, :]
                            if op == 0:
                                V.max(b[:, 0:8], s)
                            elif op == 1:
                                V.max_index(w[:, 0:8], b[:, 0:8], s)
                            elif op == 2:
                                V.match_replace(s, b[:, 0:8], s, NEG)
                            elif op == 3:
                                V.max(b[:, 8:16], s)
                            else:
                                V.max_index(w[:, 8:16], b[:, 8:16], s)
                        dve.drain()

                def candidates():
                    V.tensor_copy(tif[0:R, :, :], ti[0:R, :, :])
                    V.tensor_tensor(cand[0:R, :, :],
                                    tv[0:R, 0, :].unsqueeze(2).to_broadcast([R, TOPK, TOPK]),
                                    tv[0:R, 1:2, :].to_broadcast([R, TOPK, TOPK]), ALU.add)
                    dve.drain()
                    top16(cand[0:R, :, :].rearrange("p a b -> p (a b)"), cv[0:R, :], ci[0:R, :])
                    dve.drain()

                def positions():
                    V.tensor_scalar(shifted[0:R, :], cv[0:R, :], cv[0:R, 0:1], None, ALU.subtract
                                    ).then_inc(exp_ready, 1)
                    V.tensor_single_scalar(cpos[0:R, 0, :], ci[0:R, :], 4, ALU.logical_shift_right)
                    V.tensor_single_scalar(cpos[0:R, 1, :], ci[0:R, :], TOPK - 1, ALU.bitwise_and)
                    dve.drain()
                    V.tensor_copy(cposf[0:R, :, :], cpos[0:R, :, :])
                    dve.drain()

                def keys_of():
                    for p in range(2):
                        V.tensor_tensor(pick[0:R, p, :, :],
                                        cposf[0:R, p, :].unsqueeze(2).to_broadcast([R, TOPK, TOPK]),
                                        iota[0:R, :].unsqueeze(1).to_broadcast([R, TOPK, TOPK]), ALU.is_equal)
                    dve.drain()
                    for p in range(2):
                        V.tensor_tensor(pick[0:R, p, :, :], pick[0:R, p, :, :],
                                        tif[0:R, p:p + 1, :].to_broadcast([R, TOPK, TOPK]), ALU.mult)
                    dve.drain()
                    V.tensor_reduce(picked[0:R, :, :].rearrange("p a b -> p (a b)"),
                                    pick[0:R, :, :, :].rearrange("p a b c -> p (a b) c"), AX_X, ALU.add)
                    dve.drain()

                def finish():
                    V.scalar_tensor_tensor(out=eidx[0:R, :], in0=picked[0:R, 0, :], scalar=float(NKEYS),
                                           in1=picked[0:R, 1, :], op0=ALU.mult, op1=ALU.add)
                    dve.wait_ge(exp_done, r + 1)
                    V.reciprocal(erec[0:R, :], esum[0:R, :])
                    dve.drain()
                    V.tensor_scalar(idx[0:R, t, bass.ds(i * TOPK, TOPK)], eidx[0:R, :], float(l * EXPERTS), None,
                                    ALU.add).then_inc(routed, 1)
                    V.tensor_scalar(gate[0:R, t, bass.ds(i * TOPK, TOPK)], eexp[0:R, :], erec[0:R, 0:1], None,
                                    ALU.mult).then_inc(route_started, 1)
                    dve.drain()

                return [halves, candidates, positions, keys_of, finish]

            def gather_head(l, t, i, u, vv, beside=()):
                g = head_index(l, t) + i
                into = acc2 if t == 2 else x[t]
                gates = gate2[:, :] if t == 2 else gate[:, t, :]
                at = {2 + 3 * n: f for n, f in enumerate(beside)}
                for k in range(TOPK):
                    if u:
                        dve.wait_ge(u_landed[k % RING], 16 * (2 * g + k // RING + 1))
                        nc.vector.scalar_tensor_tensor(
                            out=uring[:, k % RING, :], in0=uring[:, k % RING, :], scalar=1.0, in1=xn[t][:, :],
                            op0=ALU.mult, op1=ALU.mult, accum_out=a_raw[:, k:k + 1]).then_inc(u_used, 1)
                    if vv:
                        n = TOPK * (g - 1) + k
                        if not (isinstance(n, int) and n == 0):
                            dve.wait_ge(v_used, n)
                        dve.wait_ge(v_landed[k % RING], 16 * (2 * (g - 1) + k // RING + 1))
                        nc.vector.scalar_tensor_tensor(
                            out=into[:, :], in0=vring[:, k % RING, :], scalar=wgt[:, k:k + 1], in1=into[:, :],
                            op0=ALU.mult, op1=ALU.add).then_inc(v_used, 1)
                    if k in at:
                        at[k]()
                if u:
                    dve.wait_ge(gelu_done, g + 1)
                    if vv:
                        dve.wait_ge(v_used, TOPK * g)
                    nc.vector.tensor_tensor(wgt[:, :], a_gelu[:, :], gates[:, bass.ds(i * TOPK, TOPK)],
                                            ALU.mult).then_inc(w_ready, 1)
                    dve.wait_ge(w_ready, g + 1)

            c1 = did(nc.vector.memset(ones[:, :], 1.0))
            c2 = did(nc.vector.memset(wsm[:, :, :], 0.0))
            c3 = did(nc.vector.memset(wsm2[:, :, :, :], 0.0))
            for l in range(LAYERS):
                if l == 0:
                    dve.wait_ge(x_landed, 16 * NT)
                dve.wait_ge(gain_landed, 32 if l == 0 else 64)
                norm(0, ROOTS_MIX[l], xn_ready)
                if l == 0:
                    dve.wait_ge(const_landed, 16 * N_CONST)
                    dve.wait_ge(ws2_landed, 16 * SB)
                    after(c3)
                    nc.vector.copy_predicated(wsm[:, :, :], tril[:, :].unsqueeze(1).to_broadcast([P, GROUPS, P]),
                                              ws[:, :, :])
                    for g in range(GROUPS):
                        nc.vector.copy_predicated(wsm2[:, g, :, :], smask[:, :, :],
                                                  ws2[:, g:g + 1, :].to_broadcast([32, SB, SS]))
                    dve.drain()
                    dve.sem_inc(ws_ready, 1)
                    for t in range(NT):
                        r = ROWS[t]
                        dve.wait_ge(scalar_read, G[("v", 3, t)][3])
                        for c in range(4):
                            n = did(nc.vector.bn_stats(stats[0:r, t, c, :], v[t][0:r, c * WCOLS:(c + 1) * WCOLS]))
                        after(n)
                        after(did(nc.vector.bn_aggr(mv[0:r, t, :], stats[0:r, t, :, :].rearrange("p a b -> p (a b)"))))
                        did(nc.vector.tensor_copy(msq[0:r, t:t + 1], mv[0:r, t, 1:2]))
                    reciprocal_roots(ROOTS_LN)
                    for t in range(NT):
                        r = ROWS[t]
                        after(did(nc.vector.tensor_scalar(v[t][0:r, :], v[t][0:r, :], mv[0:r, t, 0:1],
                                                          rstd[0:r, t:t + 1], ALU.subtract, ALU.mult)))
                        after(did(nc.vector.tensor_tensor(v[t][0:r, :], v[t][0:r, :], lng[0:r, :], ALU.mult)))
                        nc.vector.tensor_tensor(v[t][0:r, :], v[t][0:r, :], lnb[0:r, :], ALU.add
                                                ).then_inc(v_normed, 1)
                    dve.wait_ge(scalar_read, G[("u", 15)][3])
                    for b in range(16):
                        wait_group(dve, ("mix", b))
                        nc.vector.tensor_tensor(uT[:, b, :], uT[:, b, :], bank(("mix", b), TOK), ALU.mult
                                                ).then_inc(vector_read, 1)
                        dve.wait_ge(vector_read, G[("mix", b)][3])
                        dve.sem_inc(gated, 1)
                else:
                    did(nc.vector.memset(zP[:, :, 0:2], 0.0))
                    n = did(nc.vector.tensor_copy(zS[:, :, :, 0:2], state[:, :, :, :]))
                    for c in (0, 1):
                        for j in range(4):
                            k, key = 4 * c + j, ("bch", 2 * c + 1, j)
                            dve.wait_ge(scalar_read, G[("bch", 2 * c, j)][3])
                            wait_group(dve, key)
                            did(nc.vector.tensor_tensor(zP[:, k, 2:258], cT[:, k, 0:256], bank(key, 256),
                                                        ALU.mult))
                            nc.vector.tensor_tensor(
                                zS[:, k, :, 2:6], cT[:, k, 256:TOK].rearrange("p (b s) -> p b s", s=SS),
                                bank(key, 32, at=256).rearrange("p (b s) -> p b s", s=SS), ALU.mult
                            ).then_inc(vector_read, 1)
                    after(steps[0])
                    dve.wait_ge(vector_read, G[("bch", 3, 3)][3])
                    nc.vector.tensor_copy(cpn[:, :, :], zP[:, :, 256:258])
                    nc.vector.tensor_copy(csn[:, :, :, :], zS[:, :, :, 4:6])
                    dve.drain()
                    dve.sem_inc(conv_ready, 1)
                    for tap in range(3):
                        if tap:
                            after(steps[0])
                        for k in range(KD):
                            w = convw[:, tap, k:k + 1]
                            outs = (gT[:, k, 0:256], gT[:, k, 256:TOK].rearrange("p (b s) -> p b s", s=SS))
                            ins = (zP[:, k, tap:tap + 256], zS[:, k, :, tap:tap + 4])
                            for dst, src in zip(outs, ins):
                                if tap == 0:
                                    did(nc.vector.tensor_scalar(dst, src, w, None, ALU.mult))
                                else:
                                    did(nc.vector.scalar_tensor_tensor(out=dst, in0=src, scalar=w, in1=dst,
                                                                       op0=ALU.mult, op1=ALU.add))
                    after(steps[0])
                    for k in range(KD):
                        key = ("bch", 4 + k // 4, k % 4)
                        wait_group(dve, key)
                        nc.vector.tensor_tensor(gT[:, k, :], gT[:, k, :], bank(key, TOK), ALU.mult
                                                ).then_inc(vector_read, 1)
                        dve.wait_ge(vector_read, G[key][3])
                        dve.sem_inc(gated, 1)
                for n in range(2):
                    for t in range(NT):
                        add_group(("out", l, n, t), t)
                dve.wait_ge(vector_read, G[("out", l, 1, NT - 1)][3])
                norm(1, ROOTS_FFN[l], xn_ready)
                n = did(nc.vector.memset(acc2[:, :], 0.0))
                after(n)
                with dve.Fori(0, HEADS) as i:
                    for f in route(l, 0, i):
                        f()
                dve.wait_ge(xn_ready, (2 * l + 2) * NT)
                for t in range(NT):
                    if t == 2:
                        for f in range(FOLD):
                            c = f * HEADS_OF[2] * TOPK
                            nc.vector.tensor_copy(idx2[32 * f:32 * f + 32, :],
                                                  idx[0:32, 2, c:c + HEADS_OF[2] * TOPK])
                            nc.vector.tensor_copy(gate2[32 * f:32 * f + 32, :],
                                                  gate[0:32, 2, c:c + HEADS_OF[2] * TOPK])
                        dve.drain()
                        dve.sem_inc(idx2_ready, 1)
                        dve.wait_ge(xn2_spread, (FOLD - 1) * (l + 1))

                    def beside(i):
                        return route(l, t + 1, i) if t < 2 else ()

                    gather_head(l, t, 0, True, False, beside(0))
                    gather_head(l, t, 1, True, True, beside(1))
                    if HEADS_OF[t] > 2:
                        with dve.Fori(2, HEADS_OF[t]) as i:
                            gather_head(l, t, i, True, True, beside(i))
                    gather_head(l, t, HEADS_OF[t], False, True)
                dve.wait_ge(v_used, TOPK * (l + 1) * LAYER_HEADS)
                for n in range(2):
                    add_group(("fold", l, n), 2)
                dve.wait_ge(vector_read, G[("fold", l, 1)][3])
            dve.wait_ge(gain_landed, 80)
            norm(0, ROOTS_FINAL, y_ready)


_OUTS = {"y_tok": (TOK, D), "v_rows": (32, DA), "conv_prompt": (P, KD, 2), "conv_sample": (P, KD, SB, 2)}


def kernel(x_prompt, x_sample, state_conv, norm_mix, norm_ffn, norm_final,
           a_w_in, a_ln_g, a_ln_b, a_w_s, a_b_s, a_w_out,
           b_w_in, b_conv_w, b_w_out,
           peer_w_query, peer_sub_keys, peer_expert_u, peer_expert_v):
    import concourse.bacc as bacc
    from concourse.bass_utils import run_bass_kernel_spmd

    matrices = {"a_in": a_w_in[0], "a_out": a_w_out[0], "wq0": peer_w_query[0], "wq1": peer_w_query[1],
                "b_in": b_w_in[0], "b_out": b_w_out[0]}
    rows = np.arange(P)
    a = {
        "x_tok": np.concatenate([np.asarray(x_prompt).reshape(-1, D), np.asarray(x_sample).reshape(-1, D)]),
        "w_chunks": np.stack([np.asarray(matrices[m])[r:r + D, c:c + WCOLS].reshape(KD, P, WCOLS).transpose(1, 0, 2)
                              for m, c, r in CHUNKS]),
        "gains": np.stack([np.asarray(g) for g in
                           (norm_mix[0], norm_ffn[0], norm_mix[1], norm_ffn[1], norm_final)]),
        "ln_gain": np.asarray(a_ln_g),
        "ln_bias": np.asarray(a_ln_b),
        "w_s": np.asarray(a_w_s)[0].transpose(2, 0, 1),
        "b_s": np.asarray(a_b_s),
        "conv_w": np.asarray(b_conv_w)[0].reshape(3, KD, P).transpose(2, 0, 1),
        "conv_state": np.asarray(state_conv)[0].reshape(SB, 2, KD, P).transpose(3, 2, 0, 1),
        "sub_keys": np.asarray(peer_sub_keys).reshape(LAYERS, HP, NKEYS, P).transpose(0, 3, 1, 2),
        "expert_u": np.asarray(peer_expert_u).reshape(LAYERS * EXPERTS, D),
        "expert_v": np.asarray(peer_expert_v).reshape(LAYERS * EXPERTS, D),
        "ident_c": np.eye(P, dtype=np.float32),
        "iota_c": np.tile(np.arange(TOPK, dtype=np.float32), (P, 1)),
        "fold_c": (rows[:, None] % 32 == np.arange(32)[None, :]).astype(np.float32),
        "tril_c": (rows[:, None] <= rows[None, :]).astype(np.uint32),
        "smask_c": ((np.arange(32)[:, None, None] // SS == np.arange(SB)[None, :, None])
                    & (np.arange(32)[:, None, None] % SS <= np.arange(SS)[None, None, :])).astype(np.uint32),
    }
    nc = bacc.Bacc("TRN2", target_bir_lowering=False, num_devices=1)
    arrays, aps = {}, {}
    for name, arr in a.items():
        arrays[name + "_dram"] = arr = np.ascontiguousarray(arr)
        aps[name] = nc.dram_tensor(name + "_dram", arr.shape, mybir.dt.from_np(arr.dtype), kind="ExternalInput").ap()
    for name, shape in _OUTS.items():
        aps[name] = nc.dram_tensor(name + "_dram", shape, F32, kind="ExternalOutput").ap()
    trunk(nc, **aps)
    got = run_bass_kernel_spmd(nc, [arrays], core_ids=[0]).results[0]
    y = got["y_tok_dram"]
    return (y[:256].reshape(1, 256, D), y[256:].reshape(SB, SS, D),
            got["v_rows_dram"].reshape(1, SB, SS, DA),
            got["conv_prompt_dram"].transpose(2, 1, 0).reshape(1, 1, 2, D),
            got["conv_sample_dram"].transpose(2, 3, 1, 0).reshape(1, SB, 2, D))
```

```python
from contextlib import ExitStack

import numpy as np

import concourse.bass as bass
from concourse import mybir

F32 = mybir.dt.float32
U32 = mybir.dt.uint32
ALU = mybir.AluOpType
ACT = mybir.ActivationFunctionType
AX_X = mybir.AxisListType.X

P = 128
D = 1024
KD = D // P
DA = 2 * D
KA = DA // P
LAYERS = 2
NT = 3
ROWS = [128, 128, 32]
COL = [0, 128, 256]
LCOL = [0, 0, 128]
TOK = 288
PASSES = [(0, (0,)), (0, (1, 2)), (1, (0,)), (1, (1, 2))]
WIDTH = [128, 160, 128, 160]
MAXW = max(WIDTH)
SB, SS = 8, 4
HEADS, NKEYS, TOPK = 8, 128, 16
HP = 2 * HEADS
EXPERTS = NKEYS * NKEYS
GROUPS = 8
EPS = 1e-6
WCOLS = 512
HALF = 8
URING, VRING = 8, 4
FOLD = P // 32
HEADS_OF = [HEADS, HEADS, HEADS // FOLD]
HEAD0 = [0, HEADS_OF[0], HEADS_OF[0] + HEADS_OF[1]]
LAYER_HEADS = sum(HEADS_OF)
NEG = -3.0e38

LAYER_CHUNKS = [
    [("a_in", DA + c * WCOLS, 0) for c in range(4)] + [("a_in", c * WCOLS, 0) for c in range(4)]
    + [("a_out", n * WCOLS, h * D) for n in range(2) for h in range(2)]
    + [("wq0", c * WCOLS, 0) for c in range(4)],
    [("b_in", m * D + c * WCOLS, 0) for m in (1, 2, 0) for c in range(2)]
    + [("b_out", n * WCOLS, 0) for n in range(2)]
    + [("wq1", c * WCOLS, 0) for c in range(4)],
]
CHUNKS = LAYER_CHUNKS[0] + LAYER_CHUNKS[1]
LAYER_CHUNK0 = [0, len(LAYER_CHUNKS[0])]
PASS_CHUNK0 = [sum(len(LAYER_CHUNKS[l]) for l, _ in PASSES[:n]) for n in range(len(PASSES))]

ROOTS = ([("mix", 0, t) for t in range(NT)] + [("ln", 0, 0), ("ffn", 0, 0), ("ln", 0, 1), ("ln", 0, 2),
         ("ffn", 0, 1), ("ffn", 0, 2), ("mix", 1, 0), ("ffn", 1, 0), ("mix", 1, 1), ("mix", 1, 2),
         ("ffn", 1, 1), ("ffn", 1, 2)] + [("final", 1, t) for t in range(NT)])
NORMS = [("mix", 0, 0), ("mix", 0, 1), ("mix", 0, 2), ("ffn", 0, 0), ("ffn", 0, 1), ("ffn", 0, 2),
         ("mix", 1, 0), ("ffn", 1, 0), ("mix", 1, 1), ("mix", 1, 2), ("ffn", 1, 1), ("ffn", 1, 2)]


def plan_groups():
    order = []
    for n, (l, tiles) in enumerate(PASSES):
        if n == 3:
            order += [("fold", 0, c) for c in range(2)]
        order += [("xT", l, "mix", t, j) for t in tiles for j in range(2)]
        if l == 0:
            order += [("v", c, t) for c in range(4) for t in tiles]
            order += [("u", n, b) for b in range(KA)]
            order += [("mix", n, b) for b in range(KA)]
        else:
            order += [("bch", n, b) for b in range(3 * KD)]
        order += [("out", l, c, t) for c in range(2) for t in tiles]
        order += [("xT", l, "ffn", t, j) for t in tiles for j in range(2)]
        order += [("q", n, b) for b in range(HP)]
        order += [("s", l, t, j) for t in tiles for j in range(4)]
    order += [("fold", 1, c) for c in range(2)]

    groups, ranks, last, turn, banks = {}, {"vector": 0, "scalar": 0, "scores": 0}, {}, 0, 8
    for i, key in enumerate(order):
        if key[0] == "s":
            b, who, banks = (0 if key[2] == 1 else 4) + key[3], "scores", 4
        else:
            b, who = turn % banks, "vector" if key[0] in ("out", "fold") else "scalar"
            turn += 1
        ranks[who] += 1
        groups[key] = (i, b, who, ranks[who], last.get(b))
        last[b] = key
    return groups


def trunk(nc, x_tok, w_chunks, gains, ln_gain, ln_bias, w_s, b_s, conv_w, conv_state, sub_keys,
          expert_u, expert_v, ident_c, iota_c, fold_c, tril_c, smask_c,
          y_tok, v_rows, conv_prompt, conv_sample):
    G = plan_groups()
    with ExitStack() as ctx:
        def sb(name, shape, dt=F32):
            return ctx.enter_context(nc.sbuf_tensor(name, shape, dt))

        def sem(name):
            return ctx.enter_context(nc.semaphore(name))

        x = [sb(f"x{t}", [P, D]) for t in range(NT)]
        xn = [sb(f"xn{t}", [P, D]) for t in range(NT)]
        acc2 = sb("acc2", [P, D])
        xT = sb("xT", [P, KD, TOK])
        wring = sb("wring", [P, 2, KD, WCOLS])
        uring = sb("uring", [P, URING, D])
        vring = sb("vring", [P, VRING, D])
        arena = sb("arena", [P, KA * MAXW + 2 * DA + 2 * DA])
        qT = sb("qT", [P, HP, MAXW])
        keys = sb("keys", [P, HP, NKEYS])
        gain = sb("gain", [P, 2, D])
        wsm = sb("wsm", [P, GROUPS, P])
        ws2 = sb("ws2", [32, GROUPS, SS])
        wsm2 = sb("wsm2", [32, GROUPS, SB, SS])
        brow = sb("brow", [1, GROUPS, P])
        ident = sb("ident", [P, P])
        ones = sb("ones", [1, P])
        iota = sb("iota", [P, TOPK])
        fold = sb("fold", [P, 32])
        tril = sb("tril", [P, P], U32)
        zeros = sb("zeros", [P, P])
        smask = sb("smask", [32, SB, SS], U32)
        convw = sb("convw", [P, 3, KD])
        state = sb("state", [P, KD, SB, 2])
        cpn = sb("cpn", [P, KD, 2])
        csn = sb("csn", [P, KD, SB, 2])
        stats = sb("stats", [P, NT, 4, 6])
        mv = sb("mv", [P, NT, 2])
        root = sb("root", [P, NT])
        rstd = sb("rstd", [P, NT])
        msq = sb("msq", [P, NT])
        idx = sb("idx", [P, NT, HEADS * TOPK], U32)
        gate = sb("gate", [P, NT, HEADS * TOPK])
        idx2 = sb("idx2", [P, HEADS_OF[2] * TOPK], U32)
        gate2 = sb("gate2", [P, HEADS_OF[2] * TOPK])
        stage = sb("stage", [P, 2, 2, HALF], U32)
        a_raw = sb("a_raw", [P, TOPK])
        a_gelu = sb("a_gelu", [P, TOPK])
        wgt = sb("wgt", [P, TOPK])
        sh = sb("sh", [P, 2, NKEYS])
        tv = sb("tv", [P, 2, TOPK])
        ti = sb("ti", [P, 2, TOPK], U32)
        tif = sb("tif", [P, 2, TOPK])
        cand = sb("cand", [P, TOPK, TOPK])
        cv = sb("cv", [P, TOPK])
        ci = sb("ci", [P, TOPK], U32)
        cpos = sb("cpos", [P, 2, TOPK], U32)
        cposf = sb("cposf", [P, 2, TOPK])
        pick = sb("pick", [P, 2, TOPK, TOPK])
        picked = sb("picked", [P, 2, TOPK])
        eidx = sb("eidx", [P, TOPK])
        eexp = sb("eexp", [P, TOPK])
        esum = sb("esum", [P, 1])
        erec = sb("erec", [P, 1])

        o = KA * MAXW
        uT = arena[:, 0:o].rearrange("p (b t) -> p b t", t=MAXW)
        v = [arena[:, o:o + DA], arena[:, o:o + DA], arena[:, o + DA:o + 2 * DA]]
        o += 2 * DA
        lng, lnb = arena[:, o:o + DA], arena[:, o + DA:o + 2 * DA]
        mT = arena[:, o:o + KA * MAXW].rearrange("p (b t) -> p b t", t=MAXW)
        o = KD * MAXW
        cT, hT, bT, gT = (arena[:, m * o:(m + 1) * o].rearrange("p (k t) -> p k t", t=MAXW) for m in range(4))
        bchT = arena[:, 0:3 * o].rearrange("p (b t) -> p b t", t=MAXW)
        o *= 4
        zP = arena[:, o:o + KD * 258].rearrange("p (k t) -> p k t", t=258)
        o += KD * 258
        zS = arena[:, o:o + KD * SB * 6].rearrange("p (k b s) -> p k b s", b=SB, s=6)

        psum = ctx.enter_context(nc.psum_tensor("psum", [P, 8 * 512], F32))

        def bank(key, n=512, rows=P, at=0):
            b = G[key][1]
            return psum[0:rows, b * 512 + at:b * 512 + at + n]

        x_landed, const_landed, ln_landed = sem("x_landed"), sem("const_landed"), sem("ln_landed")
        gain_landed, keys_landed = sem("gain_landed"), sem("keys_landed")
        ws2_landed, ident_landed = sem("ws2_landed"), sem("ident_landed")
        w_landed = [sem(f"w_landed{r}") for r in range(2)]
        w_used = sem("w_used")
        group_done = sem("group_done")
        vector_read, scalar_read = sem("vector_read"), sem("scalar_read")
        scores_copied = sem("scores_copied")
        step = sem("step")
        xn_ready = sem("xn_ready")
        root_asked, root_taken = sem("root_asked"), sem("root_taken")
        v_normed, ws_ready, gated = sem("v_normed"), sem("ws_ready"), sem("gated")
        routed = sem("routed")
        xn2_spread, idx2_ready = sem("xn2_spread"), sem("idx2_ready")
        staged = sem("staged")
        granted, granted_act, granted_dve = sem("granted"), sem("granted_act"), sem("granted_dve")
        u_landed = [sem(f"u_landed{r}") for r in range(URING)]
        v_landed = [sem(f"v_landed{r}") for r in range(VRING)]
        u_used, v_used = sem("u_used"), sem("v_used")
        exp_done, gelu_done, w_ready = sem("exp_done"), sem("gelu_done"), sem("w_ready")
        y_ready, conv_ready = sem("y_ready"), sem("conv_ready")
        v_rows_out, conv_out, y_out = sem("v_rows_out"), sem("conv_out"), sem("y_out")

        N_CONST = 8
        block = ctx.enter_context(nc.Block())

        def route_index(l, t):
            return (l * NT + t) * HEADS

        def head_index(l, t):
            return l * LAYER_HEADS + HEAD0[t]

        def wait_group(e, key):
            e.wait_ge(group_done, G[key][0] + 1)

        @block.sync
        def _(sp):
            sp.dma_start(x[0][:, :], x_tok[0:P, :]).then_inc(x_landed, 16)
            sp.dma_start(gain[:, 0, :], gains[0:1, :].partition_broadcast(P)).then_inc(gain_landed, 16)
            sp.dma_start(ident[:, :], ident_c).then_inc(ident_landed, 16)
            for r in range(2):
                sp.dma_start(wring[:, r, :, :], w_chunks[r]).then_inc(w_landed[r], 16)
            for t in (1, 2):
                sp.dma_start(x[t][0:ROWS[t], :], x_tok[COL[t]:COL[t] + ROWS[t], :]).then_inc(x_landed, 16)
            for n, (l, _) in enumerate(PASSES):
                used, first = PASS_CHUNK0[n], LAYER_CHUNK0[l]
                if n == 2:
                    sp.wait_ge(group_done, G[("s", 0, 2, 3)][0] + 1)
                    sp.dma_start(gain[:, 0, :], gains[2:3, :].partition_broadcast(P)).then_inc(gain_landed, 16)
                    sp.dma_start(gain[:, 1, :], gains[3:4, :].partition_broadcast(P)).then_inc(gain_landed, 16)
                    sp.dma_start(keys[:, :, :], sub_keys[1]).then_inc(keys_landed, 16)
                with sp.Fori(1 if n == 0 else 0, len(LAYER_CHUNKS[l]) // 2) as i:
                    for r in range(2):
                        sp.wait_ge(w_used, used + 2 * i + r - 1)
                        sp.dma_start(wring[:, r, :, :], w_chunks[first + 2 * i + r]).then_inc(w_landed[r], 16)
            sp.wait_ge(group_done, G[("s", 1, 2, 3)][0] + 1)
            sp.dma_start(gain[:, 0, :], gains[4:5, :].partition_broadcast(P)).then_inc(gain_landed, 16)
            for t in range(NT):
                sp.wait_ge(y_ready, t + 1)
                sp.dma_start(y_tok[COL[t]:COL[t] + ROWS[t], :], xn[t][0:ROWS[t], :]).then_inc(y_out, 16)
            sp.wait_ge(y_out, 16 * NT)

        @block.gpsimd
        def _(pool):
            def half(l, t, hf, i, u, vv):
                H, g0 = HEADS_OF[t], head_index(l, t)
                source = idx2[:, :] if t == 2 else idx[:, t, :]
                if u and t < 2 and hf == 0:
                    pool.wait_ge(routed, route_index(l, t) + i + 1)
                    pool.sem_inc(granted, 1)
                if u:
                    nc.gpsimd.tensor_copy(stage[:, hf, 0, :], source[:, bass.ds(i * TOPK + hf * HALF, HALF)]
                                          ).then_inc(staged, 1)
                if vv:
                    nc.gpsimd.tensor_copy(stage[:, hf, 1, :], source[:, bass.ds((i - 1) * TOPK + hf * HALF, HALF)]
                                          ).then_inc(staged, 1)
                if u and not vv:
                    count = 1 + hf
                elif u:
                    count = 4 + (i - 1) * 4 + hf * 2
                else:
                    count = 2 + (H - 1) * 4 + hf + 1
                pool.wait_ge(staged, 4 * g0 + count)
                pool.sem_inc(granted, 1)
                for k in range(HALF):
                    n = (g0 + i) * TOPK + hf * HALF + k
                    if u:
                        if not (isinstance(n, int) and n < URING):
                            pool.wait_ge(u_used, n - URING + 1)
                            pool.sem_inc(granted, 1)
                        pool.indirect_dma_start(
                            uring[:, k % URING, :], None, expert_u,
                            bass.IndirectOffsetOnAxis(ap=stage[:, hf, 0, k:k + 1], axis=0),
                        ).then_inc(u_landed[k % URING], 16)
                    if vv:
                        n = n - TOPK
                        if not (isinstance(n, int) and n < VRING):
                            pool.wait_ge(v_used, n - VRING + 1)
                            pool.sem_inc(granted, 1)
                        pool.indirect_dma_start(
                            vring[:, k % VRING, :], None, expert_v,
                            bass.IndirectOffsetOnAxis(ap=stage[:, hf, 1, k:k + 1], axis=0),
                        ).then_inc(v_landed[k % VRING], 16)

            for l in range(LAYERS):
                for t in range(NT):
                    if t == 2:
                        pool.wait_ge(idx2_ready, l + 1)
                    H = HEADS_OF[t]
                    for hf in range(2):
                        half(l, t, hf, 0, True, False)
                    for hf in range(2):
                        half(l, t, hf, 1, True, True)
                    if H > 2:
                        with pool.Fori(2, H) as i:
                            for hf in range(2):
                                half(l, t, hf, i, True, True)
                    for hf in range(2):
                        half(l, t, hf, H, False, True)

        @block.tensor
        def _(pe):
            def open_group(key):
                before = G[key][4]
                if before is None:
                    return
                _, _, who, rank, _ = G[before]
                if who == "scores":
                    pe.wait_ge(scores_copied, route_index(before[1], before[2]) + 2 * before[3] + 2)
                else:
                    pe.wait_ge(vector_read if who == "vector" else scalar_read, rank)

            def scalar_has_read(key):
                pe.wait_ge(scalar_read, G[key][3])

            def transposes(l, which, tiles):
                for t in tiles:
                    pe.wait_ge(xn_ready, NORMS.index((which, l, t)) + 1)
                    for j in range(2):
                        key = ("xT", l, which, t, j)
                        open_group(key)
                        r = ROWS[t]
                        for m in range(4):
                            c = (4 * j + m) * P
                            last = nc.tensor.transpose(bank(key, r, at=m * P), xn[t][0:r, c:c + P],
                                                       ident[0:r, 0:r])
                        last.then_inc(group_done, 1)
                scalar_has_read(("xT", l, which, tiles[-1], 1))

            def chunk(n):
                pe.wait_ge(w_landed[n % 2], 16 * (n // 2 + 1))
                return wring[:, n % 2, :, :]

            def chunk_used(key):
                wait_group(pe, key)
                pe.sem_inc(w_used, 1)

            def blocks(n, c0, columns, name, count):
                for c in range(count // 4):
                    w = chunk(c0 + c)
                    for j in range(4):
                        key = (name, n, 4 * c + j)
                        open_group(key)
                        for k in range(KD):
                            last = nc.tensor.matmul(bank(key, WIDTH[n]), w[:, k, j * P:(j + 1) * P],
                                                    xT[:, k, columns], start=(k == 0), stop=(k == KD - 1))
                        last.then_inc(group_done, 1)
                    chunk_used(key)
                return c0 + count // 4

            def out_projection(l, tiles, c0, act, kblocks):
                per = kblocks // KD
                for c in range(2):
                    for h in range(per):
                        w = chunk(c0)
                        c0 += 1
                        for t in tiles:
                            key = ("out", l, c, t)
                            if h == 0:
                                open_group(key)
                            for k in range(KD):
                                kk = h * KD + k
                                mm = nc.tensor.matmul(bank(key, WCOLS, ROWS[t]),
                                                      act[:, kk, LCOL[t]:LCOL[t] + ROWS[t]], w[:, k, :],
                                                      start=(kk == 0), stop=(kk == kblocks - 1))
                            if h == per - 1:
                                mm.then_inc(group_done, 1)
                        if h < per - 1:
                            mm.then_inc(w_used, 1)
                        else:
                            chunk_used(key)
                return c0

            def fold_sums(l):
                pe.wait_ge(v_used, TOPK * (l + 1) * LAYER_HEADS)
                for c in range(2):
                    key = ("fold", l, c)
                    open_group(key)
                    nc.tensor.matmul(bank(key, WCOLS, 32), fold[:, :], acc2[:, c * WCOLS:(c + 1) * WCOLS],
                                     start=True, stop=True).then_inc(group_done, 1)

            pe.wait_ge(ident_landed, 16)
            for n, (l, tiles) in enumerate(PASSES):
                if n == 3:
                    fold_sums(0)
                columns = slice(COL[tiles[0]], COL[tiles[0]] + WIDTH[n])
                c0 = PASS_CHUNK0[n]
                transposes(l, "mix", tiles)
                if l == 0:
                    for c in range(4):
                        w = chunk(c0)
                        c0 += 1
                        for t in tiles:
                            key = ("v", c, t)
                            open_group(key)
                            for k in range(KD):
                                mm = nc.tensor.matmul(bank(key, WCOLS, ROWS[t]),
                                                      xT[:, k, COL[t]:COL[t] + ROWS[t]], w[:, k, :],
                                                      start=(k == 0), stop=(k == KD - 1))
                            mm.then_inc(group_done, 1)
                        chunk_used(key)
                    c0 = blocks(n, c0, columns, "u", KA)
                    pe.wait_ge(ws_ready, 1)
                    pe.wait_ge(const_landed, 16 * N_CONST)
                    pe.wait_ge(v_normed, tiles[-1] + 1)
                    for b in range(KA):
                        key, g = ("mix", n, b), b // 2
                        open_group(key)
                        for t in tiles:
                            r = ROWS[t]
                            out = bank(key, r, at=LCOL[t])
                            m = wsm[:, g, :] if t < 2 else wsm2[:, g, :, :]
                            bias = (brow[0:1, g, :] if t < 2
                                    else brow[0:1, g:g + 1, 0:SS].to_broadcast([1, SB, SS]))
                            nc.tensor.matmul(out, v[t][0:r, b * P:(b + 1) * P], m, start=True, stop=False)
                            mm = nc.tensor.matmul(out, ones[0:1, :], bias, start=False, stop=True)
                        mm.then_inc(group_done, 1)
                    pe.wait_ge(gated, n + 1)
                    c0 = out_projection(l, tiles, c0, uT, KA)
                else:
                    c0 = blocks(n, c0, columns, "bch", 3 * KD)
                    pe.wait_ge(gated, n + 1)
                    c0 = out_projection(l, tiles, c0, gT, KD)
                transposes(l, "ffn", tiles)
                blocks(n, c0, columns, "q", HP)
                pe.wait_ge(keys_landed, 16 * (l + 1))
                scalar_has_read(("q", n, HP - 1))
                for t in tiles:
                    for j in range(4):
                        key = ("s", l, t, j)
                        open_group(key)
                        for m in range(4):
                            hp = 4 * j + m
                            mm = nc.tensor.matmul(bank(key, NKEYS, ROWS[t], at=m * NKEYS),
                                                  qT[:, hp, LCOL[t]:LCOL[t] + ROWS[t]], keys[:, hp, :],
                                                  start=True, stop=True)
                        mm.then_inc(group_done, 1)
            fold_sums(1)

        @block.scalar
        def _(act):
            act.dma_start(gain[:, 1, :], gains[1:2, :].partition_broadcast(P)).then_inc(gain_landed, 16)
            act.dma_start(lng, ln_gain.partition_broadcast(P)).then_inc(ln_landed, 16)
            act.dma_start(lnb, ln_bias.partition_broadcast(P)).then_inc(ln_landed, 16)
            for dst, src in (
                (iota[:, :], iota_c), (fold[:, :], fold_c), (tril[:, :], tril_c), (smask[:, :, :], smask_c),
                (wsm[:, :, :], w_s), (brow[:, :, :], b_s), (convw[:, :, :], conv_w),
                (state[:, :, :, :], conv_state),
            ):
                act.dma_start(dst, src).then_inc(const_landed, 16)
            for b in range(SB):
                act.dma_start(ws2[SS * b:SS * b + SS, :, :], w_s[0:SS, :, 0:SS]).then_inc(ws2_landed, 16)
            act.dma_start(keys[:, :, :], sub_keys[0]).then_inc(keys_landed, 16)

            def read(key, out, func, n=512, rows=P):
                wait_group(act, key)
                nc.scalar.activation(out, bank(key, n, rows), func).then_inc(scalar_read, 1)

            def read_transposes(l, which, tiles):
                for t in tiles:
                    for j in range(2):
                        key = ("xT", l, which, t, j)
                        wait_group(act, key)
                        src = bank(key).rearrange("p (a b) -> p a b", b=P)[:, :, 0:ROWS[t]]
                        nc.scalar.copy(xT[:, 4 * j:4 * j + 4, COL[t]:COL[t] + ROWS[t]], src
                                       ).then_inc(scalar_read, 1)

            def roots(which, l, tiles):
                for t in tiles:
                    act.wait_ge(root_asked, ROOTS.index((which, l, t)) + 1)
                    nc.scalar.activation(root[0:ROWS[t], t:t + 1], root[0:ROWS[t], t:t + 1], ACT.Sqrt
                                         ).then_inc(root_taken, 1)

            def read_v(tiles):
                for c in range(4):
                    for t in tiles:
                        read(("v", c, t), v[t][0:ROWS[t], c * WCOLS:(c + 1) * WCOLS], ACT.Gelu_apprx_tanh,
                             rows=ROWS[t])

            def read_blocks(n, name, out, func, b0, b1):
                for b in range(b0, b1):
                    read((name, n, b), out[:, b, 0:WIDTH[n]], func, n=WIDTH[n])

            def spread_xn2():
                for f in range(1, FOLD):
                    nc.scalar.copy(xn[2][32 * f:32 * f + 32, :], xn[2][0:32, :]).then_inc(xn2_spread, 1)

            def weigh(l, t, i):
                g = head_index(l, t) + i
                scores = gate2[:, bass.ds(i * TOPK, TOPK)] if t == 2 else gate[:, t, bass.ds(i * TOPK, TOPK)]
                if not (isinstance(g, int) and g == 0):
                    act.wait_ge(w_ready, g)
                    act.sem_inc(granted_act, 1)
                act.wait_ge(u_used, TOPK * (g + 1))
                act.sem_inc(granted_act, 1)
                nc.scalar.activation(eexp[:, :], scores, ACT.Exp, accum_out=esum[:, :]).then_inc(exp_done, 1)
                nc.scalar.activation(a_gelu[:, :], a_raw[:, :], ACT.Gelu_apprx_tanh).then_inc(gelu_done, 1)

            roots("mix", 0, (0,))
            read_transposes(0, "mix", (0,))
            roots("mix", 0, (1, 2))
            read_v((0,))
            roots("ln", 0, (0,))
            read_blocks(0, "u", uT, ACT.Gelu_apprx_tanh, 0, KA)
            read_blocks(0, "mix", mT, ACT.Copy, 0, KA)
            roots("ffn", 0, (0,))
            read_transposes(0, "ffn", (0,))
            read_blocks(0, "q", qT, ACT.Copy, 0, HP)
            act.dma_start(lng, ln_gain.partition_broadcast(P)).then_inc(ln_landed, 16)
            act.dma_start(lnb, ln_bias.partition_broadcast(P)).then_inc(ln_landed, 16)
            read_transposes(0, "mix", (1, 2))
            read_v((1, 2))
            roots("ln", 0, (1, 2))
            weigh(0, 0, 0)
            read_blocks(1, "u", uT, ACT.Gelu_apprx_tanh, 0, KA)
            weigh(0, 0, 1)
            act.wait_ge(v_normed, NT)
            act.dma_start(v_rows, v[2][0:32, :]).then_inc(v_rows_out, 16)
            read_blocks(1, "mix", mT, ACT.Copy, 0, KA)
            weigh(0, 0, 2)
            roots("ffn", 0, (1, 2))
            weigh(0, 0, 3)
            read_transposes(0, "ffn", (1, 2))
            read_blocks(1, "q", qT, ACT.Copy, 0, HP)
            spread_xn2()
            weigh(0, 0, 4)
            with act.Fori(5, HEADS) as i:
                weigh(0, 0, i)
            roots("mix", 1, (0,))
            weigh(0, 1, 0)
            act.wait_ge(v_rows_out, 16)
            read_transposes(1, "mix", (0,))
            read_blocks(2, "bch", bchT, ACT.Copy, 0, 3 * KD)
            weigh(0, 1, 1)
            roots("ffn", 1, (0,))
            weigh(0, 1, 2)
            read_transposes(1, "ffn", (0,))
            read_blocks(2, "q", qT, ACT.Copy, 0, HP)
            weigh(0, 1, 3)
            with act.Fori(4, HEADS) as i:
                weigh(0, 1, i)
            for i in range(HEADS_OF[2]):
                weigh(0, 2, i)
            roots("mix", 1, (1, 2))
            weigh(1, 0, 0)
            read_transposes(1, "mix", (1, 2))
            read_blocks(3, "bch", bchT, ACT.Copy, 0, 2 * KD)
            weigh(1, 0, 1)
            read_blocks(3, "bch", bchT, ACT.Copy, 2 * KD, 3 * KD)
            weigh(1, 0, 2)
            roots("ffn", 1, (1, 2))
            weigh(1, 0, 3)
            read_transposes(1, "ffn", (1, 2))
            read_blocks(3, "q", qT, ACT.Copy, 0, HP)
            spread_xn2()
            act.wait_ge(conv_ready, 1)
            act.dma_start(conv_prompt, cpn[:, :, :]).then_inc(conv_out, 16)
            act.dma_start(conv_sample, csn[:, :, :, :]).then_inc(conv_out, 16)
            weigh(1, 0, 4)
            with act.Fori(5, HEADS) as i:
                weigh(1, 0, i)
            roots("final", 1, (0,))
            weigh(1, 1, 0)
            with act.Fori(1, HEADS) as i:
                weigh(1, 1, i)
            roots("final", 1, (1,))
            for i in range(HEADS_OF[2]):
                weigh(1, 2, i)
            roots("final", 1, (2,))
            act.wait_ge(conv_out, 32)

        @block.vector
        def _(dve):
            steps = [0]

            def did(instruction):
                steps[0] += 1
                instruction.then_inc(step, 1)
                return steps[0]

            def after(n):
                dve.wait_ge(step, n)

            def ask_roots(tiles):
                after(steps[0])
                for t in tiles:
                    r = ROWS[t]
                    nc.vector.tensor_scalar(root[0:r, t:t + 1], msq[0:r, t:t + 1], EPS, None, ALU.add
                                            ).then_inc(root_asked, 1)

            def rstd_of(which, l, tiles):
                for t in tiles:
                    r = ROWS[t]
                    dve.wait_ge(root_taken, ROOTS.index((which, l, t)) + 1)
                    did(nc.vector.reciprocal(rstd[0:r, t:t + 1], root[0:r, t:t + 1]))
                after(steps[0])

            def norm_stats(tiles):
                for t in tiles:
                    r = ROWS[t]
                    did(nc.vector.scalar_tensor_tensor(
                        out=xn[t][0:r, :], in0=x[t][0:r, :], scalar=1.0 / D, in1=x[t][0:r, :],
                        op0=ALU.mult, op1=ALU.mult, accum_out=msq[0:r, t:t + 1]))
                ask_roots(tiles)

            def norm_apply(which, l, tiles):
                rstd_of(which, l, tiles)
                for t in tiles:
                    r = ROWS[t]
                    nc.vector.scalar_tensor_tensor(
                        out=xn[t][0:r, :], in0=x[t][0:r, :], scalar=rstd[0:r, t:t + 1],
                        in1=gain[0:r, 1 if which == "ffn" else 0, :], op0=ALU.mult, op1=ALU.mult
                    ).then_inc(y_ready if which == "final" else xn_ready, 1)

            def add_groups(name, l, tiles):
                for c in range(2):
                    for t in tiles:
                        key = (name, l, c) if name == "fold" else (name, l, c, t)
                        wait_group(dve, key)
                        r, s = ROWS[t], slice(c * WCOLS, (c + 1) * WCOLS)
                        nc.vector.tensor_tensor(x[t][0:r, s], x[t][0:r, s], bank(key, WCOLS, r), ALU.add
                                                ).then_inc(vector_read, 1)
                dve.wait_ge(vector_read, G[key][3])

            def ln_stats(tiles):
                for t in tiles:
                    r = ROWS[t]
                    dve.wait_ge(scalar_read, G[("v", 3, t)][3])
                    for c in range(4):
                        did(nc.vector.bn_stats(stats[0:r, t, c, :], v[t][0:r, c * WCOLS:(c + 1) * WCOLS]))
                    after(steps[0])
                    after(did(nc.vector.bn_aggr(mv[0:r, t, :], stats[0:r, t, :, :].rearrange("p a b -> p (a b)"))))
                    did(nc.vector.tensor_copy(msq[0:r, t:t + 1], mv[0:r, t, 1:2]))
                ask_roots(tiles)

            def ln_apply(tiles):
                rstd_of("ln", 0, tiles)
                dve.wait_ge(ln_landed, 32 if tiles == (0,) else 64)
                for t in tiles:
                    r = ROWS[t]
                    after(did(nc.vector.tensor_scalar(v[t][0:r, :], v[t][0:r, :], mv[0:r, t, 0:1],
                                                      rstd[0:r, t:t + 1], ALU.subtract, ALU.mult)))
                    after(did(nc.vector.tensor_tensor(v[t][0:r, :], v[t][0:r, :], lng[0:r, :], ALU.mult)))
                    nc.vector.tensor_tensor(v[t][0:r, :], v[t][0:r, :], lnb[0:r, :], ALU.add
                                            ).then_inc(v_normed, 1)

            def spatial_gate(n):
                dve.wait_ge(scalar_read, G[("mix", n, KA - 1)][3])
                w = WIDTH[n]
                nc.vector.tensor_tensor(uT[:, :, 0:w], uT[:, :, 0:w], mT[:, :, 0:w], ALU.mult
                                        ).then_inc(gated, 1)

            def short_conv(n, t):
                dve.wait_ge(scalar_read, G[("bch", n, 3 * KD - 1)][3])
                samples = n == 3
                if t == 0:
                    did(nc.vector.memset(zP[:, :, 0:2], 0.0))
                did(nc.vector.tensor_tensor(zP[:, :, 2 + t * P:2 + (t + 1) * P], cT[:, :, 0:P], hT[:, :, 0:P],
                                            ALU.mult))
                if samples:
                    did(nc.vector.tensor_copy(zS[:, :, :, 0:2], state[:, :, :, :]))
                    for k in range(KD):
                        c, h = (m[:, k, P:MAXW].rearrange("p (b s) -> p b s", s=SS) for m in (cT, hT))
                        did(nc.vector.tensor_tensor(zS[:, k, :, 2:6], c, h, ALU.mult))
                after(steps[0])
                for tap in range(3):
                    for k in range(KD):
                        pairs = [(gT[:, k, 0:P], zP[:, k, t * P + tap:t * P + tap + P])]
                        if samples:
                            pairs.append((gT[:, k, P:MAXW].rearrange("p (b s) -> p b s", s=SS),
                                          zS[:, k, :, tap:tap + SS]))
                        for dst, src in pairs:
                            w = convw[:, tap, k:k + 1]
                            if tap == 0:
                                did(nc.vector.tensor_scalar(dst, src, w, None, ALU.mult))
                            else:
                                did(nc.vector.scalar_tensor_tensor(out=dst, in0=src, scalar=w, in1=dst,
                                                                   op0=ALU.mult, op1=ALU.add))
                    after(steps[0])
                w = WIDTH[n]
                nc.vector.tensor_tensor(gT[:, :, 0:w], gT[:, :, 0:w], bT[:, :, 0:w], ALU.mult).then_inc(gated, 1)
                if samples:
                    nc.vector.tensor_copy(cpn[:, :, :], zP[:, :, 256:258])
                    nc.vector.tensor_copy(csn[:, :, :, :], zS[:, :, :, 4:6])
                    dve.drain().then_inc(conv_ready, 1)

            def route(l, t, i):
                R = ROWS[t]
                V = nc.vector

                def top16(values, best, where):
                    V.max(best[:, 0:8], values)
                    dve.drain()
                    V.max_index(where[:, 0:8], best[:, 0:8], values)
                    dve.drain()
                    V.match_replace(values, best[:, 0:8], values, NEG)
                    dve.drain()
                    V.max(best[:, 8:16], values)
                    dve.drain()
                    V.max_index(where[:, 8:16], best[:, 8:16], values)

                def halves():
                    b0 = G[("s", l, t, 0)][1] * 512
                    V.tensor_copy(sh[0:R, :, :].rearrange("p a b -> p (a b)"),
                                  psum[0:R, bass.ds(b0 + i * 2 * NKEYS, 2 * NKEYS)]).then_inc(scores_copied, 1)
                    dve.drain()
                    for op in range(5):
                        for p in range(2):
                            s, b, w = sh[0:R, p, :], tv[0:R, p, :], ti[0:R, p, :]
                            if op == 0:
                                V.max(b[:, 0:8], s)
                            elif op == 1:
                                V.max_index(w[:, 0:8], b[:, 0:8], s)
                            elif op == 2:
                                V.match_replace(s, b[:, 0:8], s, NEG)
                            elif op == 3:
                                V.max(b[:, 8:16], s)
                            else:
                                V.max_index(w[:, 8:16], b[:, 8:16], s)
                        dve.drain()

                def candidates():
                    V.tensor_copy(tif[0:R, :, :], ti[0:R, :, :])
                    V.tensor_tensor(cand[0:R, :, :],
                                    tv[0:R, 0, :].unsqueeze(2).to_broadcast([R, TOPK, TOPK]),
                                    tv[0:R, 1:2, :].to_broadcast([R, TOPK, TOPK]), ALU.add)
                    dve.drain()
                    top16(cand[0:R, :, :].rearrange("p a b -> p (a b)"), cv[0:R, :], ci[0:R, :])
                    dve.drain()

                def positions():
                    V.tensor_scalar(gate[0:R, t, bass.ds(i * TOPK, TOPK)], cv[0:R, :], cv[0:R, 0:1], None,
                                    ALU.subtract)
                    V.tensor_single_scalar(cpos[0:R, 0, :], ci[0:R, :], 4, ALU.logical_shift_right)
                    V.tensor_single_scalar(cpos[0:R, 1, :], ci[0:R, :], TOPK - 1, ALU.bitwise_and)
                    dve.drain()
                    V.tensor_copy(cposf[0:R, :, :], cpos[0:R, :, :])
                    dve.drain()

                def keys_of():
                    for p in range(2):
                        V.tensor_tensor(pick[0:R, p, :, :],
                                        cposf[0:R, p, :].unsqueeze(2).to_broadcast([R, TOPK, TOPK]),
                                        iota[0:R, :].unsqueeze(1).to_broadcast([R, TOPK, TOPK]), ALU.is_equal)
                    dve.drain()
                    for p in range(2):
                        V.tensor_tensor(pick[0:R, p, :, :], pick[0:R, p, :, :],
                                        tif[0:R, p:p + 1, :].to_broadcast([R, TOPK, TOPK]), ALU.mult)
                    dve.drain()
                    V.tensor_reduce(picked[0:R, :, :].rearrange("p a b -> p (a b)"),
                                    pick[0:R, :, :, :].rearrange("p a b c -> p (a b) c"), AX_X, ALU.add)
                    dve.drain()

                def finish():
                    V.scalar_tensor_tensor(out=eidx[0:R, :], in0=picked[0:R, 0, :], scalar=float(NKEYS),
                                           in1=picked[0:R, 1, :], op0=ALU.mult, op1=ALU.add)
                    dve.drain()
                    V.tensor_scalar(idx[0:R, t, bass.ds(i * TOPK, TOPK)], eidx[0:R, :], float(l * EXPERTS), None,
                                    ALU.add).then_inc(routed, 1)

                return [halves, candidates, positions, keys_of, finish]

            def gather_head(l, t, i, u, vv, beside=None):
                g = head_index(l, t) + i
                into = acc2 if t == 2 else x[t]
                for k in range(TOPK):
                    if u:
                        dve.wait_ge(u_landed[k % URING], 16 * (TOPK // URING * g + k // URING + 1))
                        nc.vector.scalar_tensor_tensor(
                            out=uring[:, k % URING, :], in0=uring[:, k % URING, :], scalar=1.0, in1=xn[t][:, :],
                            op0=ALU.mult, op1=ALU.mult, accum_out=a_raw[:, k:k + 1]).then_inc(u_used, 1)
                    if vv:
                        n = TOPK * (g - 1) + k
                        if not (isinstance(n, int) and n == 0):
                            dve.wait_ge(v_used, n)
                        dve.wait_ge(v_landed[k % VRING], 16 * (TOPK // VRING * (g - 1) + k // VRING + 1))
                        nc.vector.scalar_tensor_tensor(
                            out=into[:, :], in0=vring[:, k % VRING, :], scalar=wgt[:, k:k + 1], in1=into[:, :],
                            op0=ALU.mult, op1=ALU.add).then_inc(v_used, 1)
                    for f in (beside or {}).get(k, ()):
                        f()
                if u:
                    dve.wait_ge(exp_done, g + 1)
                    nc.vector.reciprocal(erec[:, :], esum[:, :])
                    dve.drain()
                    dve.wait_ge(gelu_done, g + 1)
                    if vv:
                        dve.wait_ge(v_used, TOPK * g)
                    nc.vector.scalar_tensor_tensor(out=wgt[:, :], in0=a_gelu[:, :], scalar=erec[:, 0:1],
                                                   in1=eexp[:, :], op0=ALU.mult, op1=ALU.mult
                                                   ).then_inc(w_ready, 1)
                    dve.wait_ge(w_ready, g + 1)

            def heads(l, t, first, stop, routes=None, extra=None):
                def beside(i):
                    at = {k: list(f) for k, f in (extra or {}).items()}
                    for m, (rl, rt, rh) in enumerate(routes(i) if routes else ()):
                        for n, f in enumerate(route(rl, rt, rh)):
                            at.setdefault(1 + 7 * m + n, []).append(f)
                    return at

                if stop - first == 1:
                    gather_head(l, t, first, True, first > 0, beside(first))
                else:
                    with dve.Fori(first, stop) as i:
                        gather_head(l, t, i, True, True, beside(i))

            def scores_ready(l, t):
                wait_group(dve, ("s", l, t, 3))

            dve.wait_ge(x_landed, 16 * NT)
            dve.wait_ge(gain_landed, 32)
            norm_stats((0,))
            norm_apply("mix", 0, (0,))
            norm_stats((1, 2))
            norm_apply("mix", 0, (1, 2))
            did(nc.vector.memset(zeros[:, :], 0.0))
            did(nc.vector.memset(ones[:, :], 1.0))
            did(nc.vector.memset(acc2[:, :], 0.0))
            did(nc.vector.memset(wsm2[:, :, :, :], 0.0))
            dve.wait_ge(const_landed, 16 * N_CONST)
            dve.wait_ge(ws2_landed, 16 * SB)
            after(steps[0])
            for g in range(GROUPS):
                nc.vector.copy_predicated(wsm[:, g, :], tril[:, :], zeros[:, :])
                nc.vector.copy_predicated(wsm2[:, g, :, :], smask[:, :, :],
                                          ws2[:, g:g + 1, :].to_broadcast([32, SB, SS]))
            dve.drain().then_inc(ws_ready, 1)
            ln_stats((0,))
            ln_apply((0,))
            dve.wait_ge(scalar_read, G[("u", 0, KA - 1)][3])
            spatial_gate(0)
            add_groups("out", 0, (0,))
            norm_stats((0,))
            norm_apply("ffn", 0, (0,))
            scores_ready(0, 0)
            for f in route(0, 0, 0):
                f()
            dve.drain()
            dve.wait_ge(xn_ready, NORMS.index(("ffn", 0, 0)) + 1)
            heads(0, 0, 0, 1, lambda i: [(0, 0, 1), (0, 0, 2)], {15: [lambda: ln_stats((1, 2))]})
            heads(0, 0, 1, 2, lambda i: [(0, 0, 3), (0, 0, 4)], {0: [lambda: ln_apply((1, 2))]})
            heads(0, 0, 2, 3, lambda i: [(0, 0, 5), (0, 0, 6)], {6: [lambda: spatial_gate(1)]})
            heads(0, 0, 3, 4, lambda i: [(0, 0, 7)],
                  {15: [lambda: add_groups("out", 0, (1, 2)), lambda: norm_stats((1, 2))]})
            heads(0, 0, 4, 5, None, {0: [lambda: norm_apply("ffn", 0, (1, 2))]})
            scores_ready(0, 1)
            heads(0, 0, 5, HEADS, lambda i: [(0, 1, 2 * i - 10), (0, 1, 2 * i - 9)])
            gather_head(0, 0, HEADS, False, True)
            dve.wait_ge(v_used, TOPK * head_index(0, 1))
            dve.wait_ge(gain_landed, 64)
            heads(0, 1, 0, 1, lambda i: [(0, 1, 6), (0, 1, 7)], {0: [lambda: norm_stats((0,))]})
            scores_ready(0, 2)
            heads(0, 1, 1, 2, lambda i: [(0, 2, 0), (0, 2, 1)], {0: [lambda: norm_apply("mix", 1, (0,))]})
            heads(0, 1, 2, 3, lambda i: [(0, 2, 2), (0, 2, 3)],
                  {0: [lambda: short_conv(2, 0)],
                   15: [lambda: add_groups("out", 1, (0,)), lambda: norm_stats((0,))]})
            heads(0, 1, 3, 4, lambda i: [(0, 2, 4), (0, 2, 5)], {0: [lambda: norm_apply("ffn", 1, (0,))]})
            heads(0, 1, 4, 5, lambda i: [(0, 2, 6), (0, 2, 7)])
            scores_ready(1, 0)
            heads(0, 1, 5, HEADS, lambda i: [(1, 0, 2 * i - 10), (1, 0, 2 * i - 9)])

            def spread_samples():
                n = HEADS_OF[2] * TOPK
                for f in range(FOLD):
                    for dst, src in ((idx2, idx), (gate2, gate)):
                        nc.vector.tensor_copy(dst[32 * f:32 * f + 32, :], src[0:32, 2, f * n:(f + 1) * n])
                dve.drain().then_inc(idx2_ready, 1)

            spread_samples()
            gather_head(0, 1, HEADS, False, True)
            dve.wait_ge(xn2_spread, FOLD - 1)
            heads(0, 2, 0, 1, lambda i: [(1, 0, 6), (1, 0, 7)])
            heads(0, 2, 1, 2)
            gather_head(0, 2, HEADS_OF[2], False, True)
            dve.wait_ge(xn_ready, NORMS.index(("ffn", 1, 0)) + 1)
            heads(1, 0, 0, 1, None,
                  {1: [lambda: add_groups("fold", 0, (2,)), lambda: norm_stats((1, 2)),
                       lambda: did(nc.vector.memset(acc2[:, :], 0.0))]})
            heads(1, 0, 1, 2, None, {0: [lambda: norm_apply("mix", 1, (1, 2))]})
            heads(1, 0, 2, 3, None, {8: [lambda: short_conv(3, 1)]})
            heads(1, 0, 3, 4, None, {15: [lambda: add_groups("out", 1, (1, 2)), lambda: norm_stats((1, 2))]})
            heads(1, 0, 4, 5, None, {0: [lambda: norm_apply("ffn", 1, (1, 2))]})
            scores_ready(1, 1)
            heads(1, 0, 5, HEADS, lambda i: [(1, 1, 2 * i - 10), (1, 1, 2 * i - 9)])
            gather_head(1, 0, HEADS, False, True)
            dve.wait_ge(v_used, TOPK * head_index(1, 1))
            dve.wait_ge(gain_landed, 80)
            heads(1, 1, 0, 1, lambda i: [(1, 1, 6), (1, 1, 7)], {0: [lambda: norm_stats((0,))]})
            scores_ready(1, 2)
            heads(1, 1, 1, 2, lambda i: [(1, 2, 0), (1, 2, 1)], {0: [lambda: norm_apply("final", 1, (0,))]})
            heads(1, 1, 2, 5, lambda i: [(1, 2, 2 * i - 2), (1, 2, 2 * i - 1)])
            heads(1, 1, 5, HEADS)
            spread_samples()
            gather_head(1, 1, HEADS, False, True)
            dve.wait_ge(v_used, TOPK * head_index(1, 2))
            dve.wait_ge(xn2_spread, 2 * (FOLD - 1))
            heads(1, 2, 0, 1, None, {0: [lambda: norm_stats((1,))]})
            heads(1, 2, 1, 2, None, {0: [lambda: norm_apply("final", 1, (1,))]})
            gather_head(1, 2, HEADS_OF[2], False, True)
            add_groups("fold", 1, (2,))
            norm_stats((2,))
            norm_apply("final", 1, (2,))


_OUTS = {"y_tok": (TOK, D), "v_rows": (32, DA), "conv_prompt": (P, KD, 2), "conv_sample": (P, KD, SB, 2)}


def kernel(x_prompt, x_sample, state_conv, norm_mix, norm_ffn, norm_final,
           a_w_in, a_ln_g, a_ln_b, a_w_s, a_b_s, a_w_out,
           b_w_in, b_conv_w, b_w_out,
           peer_w_query, peer_sub_keys, peer_expert_u, peer_expert_v):
    import concourse.bacc as bacc
    from concourse.bass_utils import run_bass_kernel_spmd

    matrices = {"a_in": a_w_in[0], "a_out": a_w_out[0], "wq0": peer_w_query[0], "wq1": peer_w_query[1],
                "b_in": b_w_in[0], "b_out": b_w_out[0]}
    rows = np.arange(P)
    a = {
        "x_tok": np.concatenate([np.asarray(x_prompt).reshape(-1, D), np.asarray(x_sample).reshape(-1, D)]),
        "w_chunks": np.stack([np.asarray(matrices[m])[r:r + D, c:c + WCOLS].reshape(KD, P, WCOLS).transpose(1, 0, 2)
                              for m, c, r in CHUNKS]),
        "gains": np.stack([np.asarray(g) for g in
                           (norm_mix[0], norm_ffn[0], norm_mix[1], norm_ffn[1], norm_final)]),
        "ln_gain": np.asarray(a_ln_g),
        "ln_bias": np.asarray(a_ln_b),
        "w_s": np.asarray(a_w_s)[0].transpose(2, 0, 1),
        "b_s": np.asarray(a_b_s),
        "conv_w": np.asarray(b_conv_w)[0].reshape(3, KD, P).transpose(2, 0, 1),
        "conv_state": np.asarray(state_conv)[0].reshape(SB, 2, KD, P).transpose(3, 2, 0, 1),
        "sub_keys": np.asarray(peer_sub_keys).reshape(LAYERS, HP, NKEYS, P).transpose(0, 3, 1, 2),
        "expert_u": np.asarray(peer_expert_u).reshape(LAYERS * EXPERTS, D),
        "expert_v": np.asarray(peer_expert_v).reshape(LAYERS * EXPERTS, D),
        "ident_c": np.eye(P, dtype=np.float32),
        "iota_c": np.tile(np.arange(TOPK, dtype=np.float32), (P, 1)),
        "fold_c": (rows[:, None] % 32 == np.arange(32)[None, :]).astype(np.float32),
        "tril_c": (rows[:, None] > rows[None, :]).astype(np.uint32),
        "smask_c": ((np.arange(32)[:, None, None] // SS == np.arange(SB)[None, :, None])
                    & (np.arange(32)[:, None, None] % SS <= np.arange(SS)[None, None, :])).astype(np.uint32),
    }
    nc = bacc.Bacc("TRN2", target_bir_lowering=False, num_devices=1)
    arrays, aps = {}, {}
    for name, arr in a.items():
        arrays[name + "_dram"] = arr = np.ascontiguousarray(arr)
        aps[name] = nc.dram_tensor(name + "_dram", arr.shape, mybir.dt.from_np(arr.dtype), kind="ExternalInput").ap()
    for name, shape in _OUTS.items():
        aps[name] = nc.dram_tensor(name + "_dram", shape, F32, kind="ExternalOutput").ap()
    trunk(nc, **aps)
    got = run_bass_kernel_spmd(nc, [arrays], core_ids=[0]).results[0]
    y = got["y_tok_dram"]
    return (y[:256].reshape(1, 256, D), y[256:].reshape(SB, SS, D),
            got["v_rows_dram"].reshape(1, SB, SS, DA),
            got["conv_prompt_dram"].transpose(2, 1, 0).reshape(1, 1, 2, D),
            got["conv_sample_dram"].transpose(2, 3, 1, 0).reshape(1, SB, 2, D))
```

```python
from contextlib import ExitStack

import numpy as np

import concourse.bass as bass
from concourse import mybir

F32 = mybir.dt.float32
U32 = mybir.dt.uint32
ALU = mybir.AluOpType
ACT = mybir.ActivationFunctionType
AX_X = mybir.AxisListType.X

P = 128
D = 1024
KD = D // P
DA = 2 * D
KA = DA // P
LAYERS = 2
NT = 3
ROWS = [128, 128, 32]
COL = [0, 128, 256]
LCOL = [0, 0, 128]
TOK = 288
PASSES = [(0, (0,)), (0, (1, 2)), (1, (0,)), (1, (1, 2))]
WIDTH = [128, 160, 128, 160]
MAXW = max(WIDTH)
SB, SS = 8, 4
HEADS, NKEYS, TOPK = 8, 128, 16
HP = 2 * HEADS
EXPERTS = NKEYS * NKEYS
GROUPS = 8
EPS = 1e-6
WCOLS = 512
HALF = 8
URING, VRING = 8, 4
FOLD = P // 32
HEADS_OF = [HEADS, HEADS, HEADS // FOLD]
HEAD0 = [0, HEADS_OF[0], HEADS_OF[0] + HEADS_OF[1]]
LAYER_HEADS = sum(HEADS_OF)
NEG = -3.0e38

LAYER_CHUNKS = [
    [("a_in", DA + c * WCOLS, 0) for c in range(4)] + [("a_in", c * WCOLS, 0) for c in range(4)]
    + [("a_out", n * WCOLS, h * D) for n in range(2) for h in range(2)]
    + [("wq0", c * WCOLS, 0) for c in range(4)],
    [("b_in", m * D + c * WCOLS, 0) for m in (1, 2, 0) for c in range(2)]
    + [("b_out", n * WCOLS, 0) for n in range(2)]
    + [("wq1", c * WCOLS, 0) for c in range(4)],
]
CHUNKS = LAYER_CHUNKS[0] + LAYER_CHUNKS[1]
LAYER_CHUNK0 = [0, len(LAYER_CHUNKS[0])]
PASS_CHUNK0 = [sum(len(LAYER_CHUNKS[l]) for l, _ in PASSES[:n]) for n in range(len(PASSES))]

ROOTS = ([("mix", 0, t) for t in range(NT)] + [("ln", 0, 0), ("ffn", 0, 0), ("ln", 0, 1), ("ln", 0, 2),
         ("ffn", 0, 1), ("ffn", 0, 2), ("mix", 1, 0), ("ffn", 1, 0), ("mix", 1, 1), ("mix", 1, 2),
         ("ffn", 1, 1), ("ffn", 1, 2)] + [("final", 1, t) for t in range(NT)])
NORMS = [("mix", 0, 0), ("mix", 0, 1), ("mix", 0, 2), ("ffn", 0, 0), ("ffn", 0, 1), ("ffn", 0, 2),
         ("mix", 1, 0), ("ffn", 1, 0), ("mix", 1, 1), ("mix", 1, 2), ("ffn", 1, 1), ("ffn", 1, 2)]


def plan_groups():
    order = []
    for n, (l, tiles) in enumerate(PASSES):
        if n == 3:
            order += [("fold", 0, c) for c in range(2)]
        order += [("xT", l, "mix", t, j) for t in tiles for j in range(2)]
        if l == 0:
            order += [("v", c, t) for c in range(4) for t in tiles]
            order += [("u", n, b) for b in range(KA)]
            order += [("mix", n, b) for b in range(KA)]
        else:
            order += [("bch", n, b) for b in range(3 * KD)]
        order += [("out", l, c, t) for c in range(2) for t in tiles]
        order += [("xT", l, "ffn", t, j) for t in tiles for j in range(2)]
        order += [("q", n, b) for b in range(HP)]
        order += [("s", l, t, j) for t in tiles for j in range(4)]
    order += [("fold", 1, c) for c in range(2)]

    groups, ranks, last, turn, banks = {}, {"vector": 0, "scalar": 0, "scores": 0}, {}, 0, 8
    for i, key in enumerate(order):
        if key[0] == "s":
            b, who, banks = (0 if key[2] == 1 else 4) + key[3], "scores", 4
        else:
            b, who = turn % banks, "vector" if key[0] in ("out", "fold") else "scalar"
            turn += 1
        ranks[who] += 1
        groups[key] = (i, b, who, ranks[who], last.get(b))
        last[b] = key
    return groups


def trunk(nc, x_tok, w_chunks, gains, ln_gain, ln_bias, w_s, b_s, conv_w, conv_state, sub_keys,
          expert_u, expert_v, ident_c, iota_c, fold_c, tril_c, smask_c,
          y_tok, v_rows, conv_prompt, conv_sample):
    G = plan_groups()
    with ExitStack() as ctx:
        def sb(name, shape, dt=F32):
            return ctx.enter_context(nc.sbuf_tensor(name, shape, dt))

        def sem(name):
            return ctx.enter_context(nc.semaphore(name))

        x = [sb(f"x{t}", [P, D]) for t in range(NT)]
        xn = [sb(f"xn{t}", [P, D]) for t in range(NT)]
        acc2 = sb("acc2", [P, D])
        xT = sb("xT", [P, KD, TOK])
        wring = sb("wring", [P, 2, KD, WCOLS])
        uring = sb("uring", [P, URING, D])
        vring = sb("vring", [P, VRING, D])
        arena = sb("arena", [P, KA * MAXW + 2 * DA + 2 * DA])
        qT = sb("qT", [P, HP, MAXW])
        keys = sb("keys", [P, HP, NKEYS])
        gain = sb("gain", [P, 2, D])
        wsm = sb("wsm", [P, GROUPS, P])
        ws2 = sb("ws2", [32, GROUPS, SS])
        wsm2 = sb("wsm2", [32, GROUPS, SB, SS])
        brow = sb("brow", [1, GROUPS, P])
        ident = sb("ident", [P, P])
        ones = sb("ones", [1, P])
        iota = sb("iota", [P, TOPK])
        fold = sb("fold", [P, 32])
        tril = sb("tril", [P, P], U32)
        zeros = sb("zeros", [P, P])
        smask = sb("smask", [32, SB, SS], U32)
        convw = sb("convw", [P, 3, KD])
        state = sb("state", [P, KD, SB, 2])
        cpn = sb("cpn", [P, KD, 2])
        csn = sb("csn", [P, KD, SB, 2])
        stats = sb("stats", [P, NT, 4, 6])
        mv = sb("mv", [P, NT, 2])
        root = sb("root", [P, NT])
        rstd = sb("rstd", [P, NT])
        msq = sb("msq", [P, NT])
        idx = sb("idx", [P, NT, HEADS * TOPK], U32)
        gate = sb("gate", [P, NT, HEADS * TOPK])
        idx2 = sb("idx2", [P, HEADS_OF[2] * TOPK], U32)
        gate2 = sb("gate2", [P, HEADS_OF[2] * TOPK])
        stage = sb("stage", [P, 2, 2, HALF], U32)
        a_raw = sb("a_raw", [P, TOPK])
        a_gelu = sb("a_gelu", [P, TOPK])
        wgt = sb("wgt", [P, TOPK])
        pick = sb("pick", [P, 4 * TOPK, TOPK])
        work = pick[:, :, :].rearrange("p a b -> p (a b)")
        sh = work[:, 0:4 * NKEYS].rearrange("p (a b) -> p a b", b=NKEYS)
        cand = work[:, 4 * NKEYS:8 * NKEYS].rearrange("p (m a b) -> p m a b", a=TOPK, b=TOPK)
        tv = sb("tv", [P, 4, TOPK])
        ti = sb("ti", [P, 4, TOPK], U32)
        tif = sb("tif", [P, 4, TOPK])
        cv = sb("cv", [P, 2, TOPK])
        ci = sb("ci", [P, 2, TOPK], U32)
        cpos = sb("cpos", [P, 2, 2, TOPK], U32)
        cposf = sb("cposf", [P, 4 * TOPK])
        picked = sb("picked", [P, 2, 2, TOPK])
        eidx = sb("eidx", [P, 2, TOPK])
        eexp = sb("eexp", [P, TOPK])
        esum = sb("esum", [P, 1])
        erec = sb("erec", [P, 1])

        o = KA * MAXW
        uT = arena[:, 0:o].rearrange("p (b t) -> p b t", t=MAXW)
        v = [arena[:, o:o + DA], arena[:, o:o + DA], arena[:, o + DA:o + 2 * DA]]
        o += 2 * DA
        lng, lnb = arena[:, o:o + DA], arena[:, o + DA:o + 2 * DA]
        mT = arena[:, o:o + KA * MAXW].rearrange("p (b t) -> p b t", t=MAXW)
        o = KD * MAXW
        cT, hT, bT, gT = (arena[:, m * o:(m + 1) * o].rearrange("p (k t) -> p k t", t=MAXW) for m in range(4))
        bchT = arena[:, 0:3 * o].rearrange("p (b t) -> p b t", t=MAXW)
        o *= 4
        zP = arena[:, o:o + KD * 258].rearrange("p (k t) -> p k t", t=258)
        o += KD * 258
        zS = arena[:, o:o + KD * SB * 6].rearrange("p (k b s) -> p k b s", b=SB, s=6)

        psum = ctx.enter_context(nc.psum_tensor("psum", [P, 8 * 512], F32))

        def bank(key, n=512, rows=P, at=0):
            b = G[key][1]
            return psum[0:rows, b * 512 + at:b * 512 + at + n]

        x_landed, const_landed, ln_landed = sem("x_landed"), sem("const_landed"), sem("ln_landed")
        gain_landed, keys_landed = sem("gain_landed"), sem("keys_landed")
        ws2_landed, ident_landed = sem("ws2_landed"), sem("ident_landed")
        w_landed = [sem(f"w_landed{r}") for r in range(2)]
        w_used = sem("w_used")
        group_done = sem("group_done")
        vector_read, scalar_read = sem("vector_read"), sem("scalar_read")
        scores_copied = sem("scores_copied")
        step = sem("step")
        xn_ready = sem("xn_ready")
        root_asked, root_taken = sem("root_asked"), sem("root_taken")
        v_normed, ws_ready, gated = sem("v_normed"), sem("ws_ready"), sem("gated")
        routed = sem("routed")
        xn2_spread, idx2_ready = sem("xn2_spread"), sem("idx2_ready")
        staged = sem("staged")
        granted, granted_act, granted_dve = sem("granted"), sem("granted_act"), sem("granted_dve")
        u_landed = [sem(f"u_landed{r}") for r in range(URING)]
        v_landed = [sem(f"v_landed{r}") for r in range(VRING)]
        u_used, v_used = sem("u_used"), sem("v_used")
        exp_done, w_ready = sem("exp_done"), sem("w_ready")
        gelu_half_done, gelu_done = sem("gelu_half_done"), sem("gelu_done")
        y_ready, conv_ready = sem("y_ready"), sem("conv_ready")
        v_rows_out, conv_out, y_out = sem("v_rows_out"), sem("conv_out"), sem("y_out")

        N_CONST = 8
        block = ctx.enter_context(nc.Block())

        def route_index(l, t):
            return (l * NT + t) * HEADS

        def head_index(l, t):
            return l * LAYER_HEADS + HEAD0[t]

        def wait_group(e, key):
            e.wait_ge(group_done, G[key][0] + 1)

        @block.sync
        def _(sp):
            sp.dma_start(x[0][:, :], x_tok[0:P, :]).then_inc(x_landed, 16)
            sp.dma_start(gain[:, 0, :], gains[0:1, :].partition_broadcast(P)).then_inc(gain_landed, 16)
            sp.dma_start(ident[:, :], ident_c).then_inc(ident_landed, 16)
            for r in range(2):
                sp.dma_start(wring[:, r, :, :], w_chunks[r]).then_inc(w_landed[r], 16)
            for t in (1, 2):
                sp.dma_start(x[t][0:ROWS[t], :], x_tok[COL[t]:COL[t] + ROWS[t], :]).then_inc(x_landed, 16)
            for n, (l, _) in enumerate(PASSES):
                used, first = PASS_CHUNK0[n], LAYER_CHUNK0[l]
                if n == 2:
                    sp.wait_ge(group_done, G[("s", 0, 2, 3)][0] + 1)
                    sp.dma_start(gain[:, 0, :], gains[2:3, :].partition_broadcast(P)).then_inc(gain_landed, 16)
                    sp.dma_start(gain[:, 1, :], gains[3:4, :].partition_broadcast(P)).then_inc(gain_landed, 16)
                    sp.dma_start(keys[:, :, :], sub_keys[1]).then_inc(keys_landed, 16)
                with sp.Fori(1 if n == 0 else 0, len(LAYER_CHUNKS[l]) // 2) as i:
                    for r in range(2):
                        sp.wait_ge(w_used, used + 2 * i + r - 1)
                        sp.dma_start(wring[:, r, :, :], w_chunks[first + 2 * i + r]).then_inc(w_landed[r], 16)
            sp.wait_ge(group_done, G[("s", 1, 2, 3)][0] + 1)
            sp.dma_start(gain[:, 0, :], gains[4:5, :].partition_broadcast(P)).then_inc(gain_landed, 16)
            for t in range(NT):
                sp.wait_ge(y_ready, t + 1)
                sp.dma_start(y_tok[COL[t]:COL[t] + ROWS[t], :], xn[t][0:ROWS[t], :]).then_inc(y_out, 16)
            sp.wait_ge(y_out, 16 * NT)

        @block.gpsimd
        def _(pool):
            def half(l, t, hf, i, u, vv):
                H, g0 = HEADS_OF[t], head_index(l, t)
                source = idx2[:, :] if t == 2 else idx[:, t, :]
                if u and t < 2 and hf == 0:
                    pool.wait_ge(routed, route_index(l, t) + i + 1)
                    pool.sem_inc(granted, 1)
                if u:
                    nc.gpsimd.tensor_copy(stage[:, hf, 0, :], source[:, bass.ds(i * TOPK + hf * HALF, HALF)]
                                          ).then_inc(staged, 1)
                if vv:
                    nc.gpsimd.tensor_copy(stage[:, hf, 1, :], source[:, bass.ds((i - 1) * TOPK + hf * HALF, HALF)]
                                          ).then_inc(staged, 1)
                if u and not vv:
                    count = 1 + hf
                elif u:
                    count = 4 + (i - 1) * 4 + hf * 2
                else:
                    count = 2 + (H - 1) * 4 + hf + 1
                pool.wait_ge(staged, 4 * g0 + count)
                pool.sem_inc(granted, 1)
                for k in range(HALF):
                    n = (g0 + i) * TOPK + hf * HALF + k
                    if u:
                        if not (isinstance(n, int) and n < URING):
                            pool.wait_ge(u_used, n - URING + 1)
                            pool.sem_inc(granted, 1)
                        pool.indirect_dma_start(
                            uring[:, k % URING, :], None, expert_u,
                            bass.IndirectOffsetOnAxis(ap=stage[:, hf, 0, k:k + 1], axis=0),
                        ).then_inc(u_landed[k % URING], 16)
                    if vv:
                        n = n - TOPK
                        if not (isinstance(n, int) and n < VRING):
                            pool.wait_ge(v_used, n - VRING + 1)
                            pool.sem_inc(granted, 1)
                        pool.indirect_dma_start(
                            vring[:, k % VRING, :], None, expert_v,
                            bass.IndirectOffsetOnAxis(ap=stage[:, hf, 1, k:k + 1], axis=0),
                        ).then_inc(v_landed[k % VRING], 16)

            for l in range(LAYERS):
                for t in range(NT):
                    if t == 2:
                        pool.wait_ge(idx2_ready, l + 1)
                    H = HEADS_OF[t]
                    for hf in range(2):
                        half(l, t, hf, 0, True, False)
                    for hf in range(2):
                        half(l, t, hf, 1, True, True)
                    if H > 2:
                        with pool.Fori(2, H) as i:
                            for hf in range(2):
                                half(l, t, hf, i, True, True)
                    for hf in range(2):
                        half(l, t, hf, H, False, True)

        @block.tensor
        def _(pe):
            def open_group(key):
                before = G[key][4]
                if before is None:
                    return
                _, _, who, rank, _ = G[before]
                if who == "scores":
                    pe.wait_ge(scores_copied, route_index(before[1], before[2]) + 2 * before[3] + 2)
                else:
                    pe.wait_ge(vector_read if who == "vector" else scalar_read, rank)

            def scalar_has_read(key):
                pe.wait_ge(scalar_read, G[key][3])

            def transposes(l, which, tiles):
                for t in tiles:
                    pe.wait_ge(xn_ready, NORMS.index((which, l, t)) + 1)
                    for j in range(2):
                        key = ("xT", l, which, t, j)
                        open_group(key)
                        r = ROWS[t]
                        for m in range(4):
                            c = (4 * j + m) * P
                            last = nc.tensor.transpose(bank(key, r, at=m * P), xn[t][0:r, c:c + P],
                                                       ident[0:r, 0:r])
                        last.then_inc(group_done, 1)
                scalar_has_read(("xT", l, which, tiles[-1], 1))

            def chunk(n):
                pe.wait_ge(w_landed[n % 2], 16 * (n // 2 + 1))
                return wring[:, n % 2, :, :]

            def chunk_used(key):
                wait_group(pe, key)
                pe.sem_inc(w_used, 1)

            def blocks(n, c0, columns, name, count):
                for c in range(count // 4):
                    w = chunk(c0 + c)
                    for j in range(4):
                        key = (name, n, 4 * c + j)
                        open_group(key)
                        for k in range(KD):
                            last = nc.tensor.matmul(bank(key, WIDTH[n]), w[:, k, j * P:(j + 1) * P],
                                                    xT[:, k, columns], start=(k == 0), stop=(k == KD - 1))
                        last.then_inc(group_done, 1)
                    chunk_used(key)
                return c0 + count // 4

            def out_projection(l, tiles, c0, act, kblocks):
                per = kblocks // KD
                for c in range(2):
                    for h in range(per):
                        w = chunk(c0)
                        c0 += 1
                        for t in tiles:
                            key = ("out", l, c, t)
                            if h == 0:
                                open_group(key)
                            for k in range(KD):
                                kk = h * KD + k
                                mm = nc.tensor.matmul(bank(key, WCOLS, ROWS[t]),
                                                      act[:, kk, LCOL[t]:LCOL[t] + ROWS[t]], w[:, k, :],
                                                      start=(kk == 0), stop=(kk == kblocks - 1))
                            if h == per - 1:
                                mm.then_inc(group_done, 1)
                        if h < per - 1:
                            mm.then_inc(w_used, 1)
                        else:
                            chunk_used(key)
                return c0

            def fold_sums(l):
                pe.wait_ge(v_used, TOPK * (l + 1) * LAYER_HEADS)
                for c in range(2):
                    key = ("fold", l, c)
                    open_group(key)
                    nc.tensor.matmul(bank(key, WCOLS, 32), fold[:, :], acc2[:, c * WCOLS:(c + 1) * WCOLS],
                                     start=True, stop=True).then_inc(group_done, 1)

            pe.wait_ge(ident_landed, 16)
            for n, (l, tiles) in enumerate(PASSES):
                if n == 3:
                    fold_sums(0)
                columns = slice(COL[tiles[0]], COL[tiles[0]] + WIDTH[n])
                c0 = PASS_CHUNK0[n]
                transposes(l, "mix", tiles)
                if l == 0:
                    for c in range(4):
                        w = chunk(c0)
                        c0 += 1
                        for t in tiles:
                            key = ("v", c, t)
                            open_group(key)
                            for k in range(KD):
                                mm = nc.tensor.matmul(bank(key, WCOLS, ROWS[t]),
                                                      xT[:, k, COL[t]:COL[t] + ROWS[t]], w[:, k, :],
                                                      start=(k == 0), stop=(k == KD - 1))
                            mm.then_inc(group_done, 1)
                        chunk_used(key)
                    c0 = blocks(n, c0, columns, "u", KA)
                    pe.wait_ge(ws_ready, 1)
                    pe.wait_ge(const_landed, 16 * N_CONST)
                    pe.wait_ge(v_normed, tiles[-1] + 1)
                    for b in range(KA):
                        key, g = ("mix", n, b), b // 2
                        open_group(key)
                        for t in tiles:
                            r = ROWS[t]
                            out = bank(key, r, at=LCOL[t])
                            m = wsm[:, g, :] if t < 2 else wsm2[:, g, :, :]
                            bias = (brow[0:1, g, :] if t < 2
                                    else brow[0:1, g:g + 1, 0:SS].to_broadcast([1, SB, SS]))
                            nc.tensor.matmul(out, v[t][0:r, b * P:(b + 1) * P], m, start=True, stop=False)
                            mm = nc.tensor.matmul(out, ones[0:1, :], bias, start=False, stop=True)
                        mm.then_inc(group_done, 1)
                    pe.wait_ge(gated, n + 1)
                    c0 = out_projection(l, tiles, c0, uT, KA)
                else:
                    c0 = blocks(n, c0, columns, "bch", 3 * KD)
                    pe.wait_ge(gated, n + 1)
                    c0 = out_projection(l, tiles, c0, gT, KD)
                transposes(l, "ffn", tiles)
                blocks(n, c0, columns, "q", HP)
                pe.wait_ge(keys_landed, 16 * (l + 1))
                scalar_has_read(("q", n, HP - 1))
                for t in tiles:
                    for j in range(4):
                        key = ("s", l, t, j)
                        open_group(key)
                        for m in range(4):
                            hp = 4 * j + m
                            mm = nc.tensor.matmul(bank(key, NKEYS, ROWS[t], at=m * NKEYS),
                                                  qT[:, hp, LCOL[t]:LCOL[t] + ROWS[t]], keys[:, hp, :],
                                                  start=True, stop=True)
                        mm.then_inc(group_done, 1)
            fold_sums(1)

        @block.scalar
        def _(act):
            act.dma_start(gain[:, 1, :], gains[1:2, :].partition_broadcast(P)).then_inc(gain_landed, 16)
            act.dma_start(lng, ln_gain.partition_broadcast(P)).then_inc(ln_landed, 16)
            act.dma_start(lnb, ln_bias.partition_broadcast(P)).then_inc(ln_landed, 16)
            for dst, src in (
                (iota[:, :], iota_c), (fold[:, :], fold_c), (tril[:, :], tril_c), (smask[:, :, :], smask_c),
                (wsm[:, :, :], w_s), (brow[:, :, :], b_s), (convw[:, :, :], conv_w),
                (state[:, :, :, :], conv_state),
            ):
                act.dma_start(dst, src).then_inc(const_landed, 16)
            for b in range(SB):
                act.dma_start(ws2[SS * b:SS * b + SS, :, :], w_s[0:SS, :, 0:SS]).then_inc(ws2_landed, 16)
            act.dma_start(keys[:, :, :], sub_keys[0]).then_inc(keys_landed, 16)

            def read(key, out, func, n=512, rows=P):
                wait_group(act, key)
                nc.scalar.activation(out, bank(key, n, rows), func).then_inc(scalar_read, 1)

            def read_transposes(l, which, tiles):
                for t in tiles:
                    for j in range(2):
                        key = ("xT", l, which, t, j)
                        wait_group(act, key)
                        src = bank(key).rearrange("p (a b) -> p a b", b=P)[:, :, 0:ROWS[t]]
                        nc.scalar.copy(xT[:, 4 * j:4 * j + 4, COL[t]:COL[t] + ROWS[t]], src
                                       ).then_inc(scalar_read, 1)

            def roots(which, l, tiles):
                for t in tiles:
                    act.wait_ge(root_asked, ROOTS.index((which, l, t)) + 1)
                    nc.scalar.activation(root[0:ROWS[t], t:t + 1], root[0:ROWS[t], t:t + 1], ACT.Sqrt
                                         ).then_inc(root_taken, 1)

            def read_v(tiles):
                for c in range(4):
                    for t in tiles:
                        read(("v", c, t), v[t][0:ROWS[t], c * WCOLS:(c + 1) * WCOLS], ACT.Gelu_apprx_tanh,
                             rows=ROWS[t])

            def read_blocks(n, name, out, func, b0, b1):
                for b in range(b0, b1):
                    read((name, n, b), out[:, b, 0:WIDTH[n]], func, n=WIDTH[n])

            def spread_xn2():
                for f in range(1, FOLD):
                    nc.scalar.copy(xn[2][32 * f:32 * f + 32, :], xn[2][0:32, :]).then_inc(xn2_spread, 1)

            def weigh(l, t, i):
                g = head_index(l, t) + i
                scores = gate2[:, bass.ds(i * TOPK, TOPK)] if t == 2 else gate[:, t, bass.ds(i * TOPK, TOPK)]
                if not (isinstance(g, int) and g == 0):
                    act.wait_ge(w_ready, g)
                    act.sem_inc(granted_act, 1)
                if t == 2:
                    act.wait_ge(idx2_ready, l + 1)
                else:
                    act.wait_ge(routed, route_index(l, t) + i + 1)
                    act.sem_inc(granted_act, 1)
                nc.scalar.activation(eexp[:, :], scores, ACT.Exp, accum_out=esum[:, :]).then_inc(exp_done, 1)
                for h, done in enumerate((gelu_half_done, gelu_done)):
                    act.wait_ge(u_used, TOPK * g + (h + 1) * HALF)
                    act.sem_inc(granted_act, 1)
                    c = slice(h * HALF, (h + 1) * HALF)
                    nc.scalar.activation(a_gelu[:, c], a_raw[:, c], ACT.Gelu_apprx_tanh).then_inc(done, 1)

            roots("mix", 0, (0,))
            read_transposes(0, "mix", (0,))
            roots("mix", 0, (1, 2))
            read_v((0,))
            roots("ln", 0, (0,))
            read_blocks(0, "u", uT, ACT.Gelu_apprx_tanh, 0, KA)
            read_blocks(0, "mix", mT, ACT.Copy, 0, KA)
            roots("ffn", 0, (0,))
            read_transposes(0, "ffn", (0,))
            read_blocks(0, "q", qT, ACT.Copy, 0, HP)
            act.dma_start(lng, ln_gain.partition_broadcast(P)).then_inc(ln_landed, 16)
            act.dma_start(lnb, ln_bias.partition_broadcast(P)).then_inc(ln_landed, 16)
            read_transposes(0, "mix", (1, 2))
            read_v((1, 2))
            roots("ln", 0, (1, 2))
            weigh(0, 0, 0)
            read_blocks(1, "u", uT, ACT.Gelu_apprx_tanh, 0, KA)
            weigh(0, 0, 1)
            act.wait_ge(v_normed, NT)
            act.dma_start(v_rows, v[2][0:32, :]).then_inc(v_rows_out, 16)
            read_blocks(1, "mix", mT, ACT.Copy, 0, KA)
            weigh(0, 0, 2)
            roots("ffn", 0, (1, 2))
            weigh(0, 0, 3)
            read_transposes(0, "ffn", (1, 2))
            read_blocks(1, "q", qT, ACT.Copy, 0, HP)
            spread_xn2()
            weigh(0, 0, 4)
            with act.Fori(5, HEADS) as i:
                weigh(0, 0, i)
            roots("mix", 1, (0,))
            weigh(0, 1, 0)
            act.wait_ge(v_rows_out, 16)
            read_transposes(1, "mix", (0,))
            read_blocks(2, "bch", bchT, ACT.Copy, 0, 3 * KD)
            weigh(0, 1, 1)
            roots("ffn", 1, (0,))
            weigh(0, 1, 2)
            read_transposes(1, "ffn", (0,))
            read_blocks(2, "q", qT, ACT.Copy, 0, HP)
            weigh(0, 1, 3)
            with act.Fori(4, HEADS) as i:
                weigh(0, 1, i)
            for i in range(HEADS_OF[2]):
                weigh(0, 2, i)
            roots("mix", 1, (1, 2))
            weigh(1, 0, 0)
            read_transposes(1, "mix", (1, 2))
            read_blocks(3, "bch", bchT, ACT.Copy, 0, 2 * KD)
            weigh(1, 0, 1)
            read_blocks(3, "bch", bchT, ACT.Copy, 2 * KD, 3 * KD)
            weigh(1, 0, 2)
            roots("ffn", 1, (1, 2))
            weigh(1, 0, 3)
            read_transposes(1, "ffn", (1, 2))
            read_blocks(3, "q", qT, ACT.Copy, 0, HP)
            spread_xn2()
            act.wait_ge(conv_ready, 1)
            act.dma_start(conv_prompt, cpn[:, :, :]).then_inc(conv_out, 16)
            act.dma_start(conv_sample, csn[:, :, :, :]).then_inc(conv_out, 16)
            weigh(1, 0, 4)
            with act.Fori(5, HEADS) as i:
                weigh(1, 0, i)
            roots("final", 1, (0,))
            weigh(1, 1, 0)
            with act.Fori(1, HEADS) as i:
                weigh(1, 1, i)
            roots("final", 1, (1,))
            for i in range(HEADS_OF[2]):
                weigh(1, 2, i)
            roots("final", 1, (2,))
            act.wait_ge(conv_out, 32)

        @block.vector
        def _(dve):
            steps = [0]

            def did(instruction):
                steps[0] += 1
                instruction.then_inc(step, 1)
                return steps[0]

            def after(n):
                dve.wait_ge(step, n)

            def ask_roots(tiles):
                after(steps[0])
                for t in tiles:
                    r = ROWS[t]
                    nc.vector.tensor_scalar(root[0:r, t:t + 1], msq[0:r, t:t + 1], EPS, None, ALU.add
                                            ).then_inc(root_asked, 1)

            def rstd_of(which, l, tiles):
                for t in tiles:
                    r = ROWS[t]
                    dve.wait_ge(root_taken, ROOTS.index((which, l, t)) + 1)
                    did(nc.vector.reciprocal(rstd[0:r, t:t + 1], root[0:r, t:t + 1]))
                after(steps[0])

            def norm_stats(tiles):
                for t in tiles:
                    r = ROWS[t]
                    did(nc.vector.scalar_tensor_tensor(
                        out=xn[t][0:r, :], in0=x[t][0:r, :], scalar=1.0 / D, in1=x[t][0:r, :],
                        op0=ALU.mult, op1=ALU.mult, accum_out=msq[0:r, t:t + 1]))
                ask_roots(tiles)

            def norm_apply(which, l, tiles):
                rstd_of(which, l, tiles)
                for t in tiles:
                    r = ROWS[t]
                    nc.vector.scalar_tensor_tensor(
                        out=xn[t][0:r, :], in0=x[t][0:r, :], scalar=rstd[0:r, t:t + 1],
                        in1=gain[0:r, 1 if which == "ffn" else 0, :], op0=ALU.mult, op1=ALU.mult
                    ).then_inc(y_ready if which == "final" else xn_ready, 1)

            def add_groups(name, l, tiles):
                for c in range(2):
                    for t in tiles:
                        key = (name, l, c) if name == "fold" else (name, l, c, t)
                        wait_group(dve, key)
                        r, s = ROWS[t], slice(c * WCOLS, (c + 1) * WCOLS)
                        nc.vector.tensor_tensor(x[t][0:r, s], x[t][0:r, s], bank(key, WCOLS, r), ALU.add
                                                ).then_inc(vector_read, 1)
                dve.wait_ge(vector_read, G[key][3])

            def ln_stats(tiles):
                for t in tiles:
                    r = ROWS[t]
                    dve.wait_ge(scalar_read, G[("v", 3, t)][3])
                    for c in range(4):
                        did(nc.vector.bn_stats(stats[0:r, t, c, :], v[t][0:r, c * WCOLS:(c + 1) * WCOLS]))
                    after(steps[0])
                    after(did(nc.vector.bn_aggr(mv[0:r, t, :], stats[0:r, t, :, :].rearrange("p a b -> p (a b)"))))
                    did(nc.vector.tensor_copy(msq[0:r, t:t + 1], mv[0:r, t, 1:2]))
                ask_roots(tiles)

            def ln_apply(tiles):
                rstd_of("ln", 0, tiles)
                dve.wait_ge(ln_landed, 32 if tiles == (0,) else 64)
                for t in tiles:
                    r = ROWS[t]
                    after(did(nc.vector.tensor_scalar(v[t][0:r, :], v[t][0:r, :], mv[0:r, t, 0:1],
                                                      rstd[0:r, t:t + 1], ALU.subtract, ALU.mult)))
                    after(did(nc.vector.tensor_tensor(v[t][0:r, :], v[t][0:r, :], lng[0:r, :], ALU.mult)))
                    nc.vector.tensor_tensor(v[t][0:r, :], v[t][0:r, :], lnb[0:r, :], ALU.add
                                            ).then_inc(v_normed, 1)

            def spatial_gate(n):
                dve.wait_ge(scalar_read, G[("mix", n, KA - 1)][3])
                w = WIDTH[n]
                nc.vector.tensor_tensor(uT[:, :, 0:w], uT[:, :, 0:w], mT[:, :, 0:w], ALU.mult
                                        ).then_inc(gated, 1)

            def short_conv(n, t):
                dve.wait_ge(scalar_read, G[("bch", n, 3 * KD - 1)][3])
                samples = n == 3
                if t == 0:
                    did(nc.vector.memset(zP[:, :, 0:2], 0.0))
                did(nc.vector.tensor_tensor(zP[:, :, 2 + t * P:2 + (t + 1) * P], cT[:, :, 0:P], hT[:, :, 0:P],
                                            ALU.mult))
                if samples:
                    did(nc.vector.tensor_copy(zS[:, :, :, 0:2], state[:, :, :, :]))
                    for k in range(KD):
                        c, h = (m[:, k, P:MAXW].rearrange("p (b s) -> p b s", s=SS) for m in (cT, hT))
                        did(nc.vector.tensor_tensor(zS[:, k, :, 2:6], c, h, ALU.mult))
                after(steps[0])
                for tap in range(3):
                    for k in range(KD):
                        pairs = [(gT[:, k, 0:P], zP[:, k, t * P + tap:t * P + tap + P])]
                        if samples:
                            pairs.append((gT[:, k, P:MAXW].rearrange("p (b s) -> p b s", s=SS),
                                          zS[:, k, :, tap:tap + SS]))
                        for dst, src in pairs:
                            w = convw[:, tap, k:k + 1]
                            if tap == 0:
                                did(nc.vector.tensor_scalar(dst, src, w, None, ALU.mult))
                            else:
                                did(nc.vector.scalar_tensor_tensor(out=dst, in0=src, scalar=w, in1=dst,
                                                                   op0=ALU.mult, op1=ALU.add))
                    after(steps[0])
                w = WIDTH[n]
                nc.vector.tensor_tensor(gT[:, :, 0:w], gT[:, :, 0:w], bT[:, :, 0:w], ALU.mult).then_inc(gated, 1)
                if samples:
                    nc.vector.tensor_copy(cpn[:, :, :], zP[:, :, 256:258])
                    nc.vector.tensor_copy(csn[:, :, :, :], zS[:, :, :, 4:6])
                    dve.drain().then_inc(conv_ready, 1)

            def route(l, t, i):
                R = ROWS[t]
                V = nc.vector
                sides = [(sh[0:R, m, :], tv[0:R, m, :], ti[0:R, m, :]) for m in range(4)]
                both = [(cand[0:R, m, :, :].rearrange("p a b -> p (a b)"), cv[0:R, m, :], ci[0:R, m, :])
                        for m in range(2)]

                def copy_scores():
                    b0 = G[("s", l, t, 0)][1] * 512
                    V.tensor_copy(sh[0:R, :, :].rearrange("p a b -> p (a b)"),
                                  psum[0:R, bass.ds(b0 + i * 2 * NKEYS, 4 * NKEYS)]).then_inc(scores_copied, 2)
                    dve.drain()

                def first8(lists):
                    for values, best, _ in lists:
                        V.max(best[:, 0:8], values)
                    dve.drain()
                    for values, best, where in lists:
                        V.max_index(where[:, 0:8], best[:, 0:8], values)
                    dve.drain()

                def next8(lists):
                    for values, best, _ in lists:
                        V.match_replace(values, best[:, 0:8], values, NEG)
                    dve.drain()
                    for values, best, _ in lists:
                        V.max(best[:, 8:16], values)
                    dve.drain()
                    for values, best, where in lists:
                        V.max_index(where[:, 8:16], best[:, 8:16], values)

                def candidates():
                    dve.drain()
                    V.tensor_copy(tif[0:R, :, :], ti[0:R, :, :])
                    for m in range(2):
                        V.tensor_tensor(cand[0:R, m, :, :],
                                        tv[0:R, 2 * m, :].unsqueeze(2).to_broadcast([R, TOPK, TOPK]),
                                        tv[0:R, 2 * m + 1:2 * m + 2, :].to_broadcast([R, TOPK, TOPK]), ALU.add)
                    dve.drain()

                def positions():
                    dve.drain()
                    V.tensor_tensor(gate[0:R, t, bass.ds(i * TOPK, 2 * TOPK)].rearrange("p (a b) -> p a b", b=TOPK),
                                    cv[0:R, :, :], cv[0:R, :, 0:1].to_broadcast([R, 2, TOPK]), ALU.subtract)
                    V.tensor_single_scalar(cpos[0:R, :, 0, :], ci[0:R, :, :], 4, ALU.logical_shift_right)
                    V.tensor_single_scalar(cpos[0:R, :, 1, :], ci[0:R, :, :], TOPK - 1, ALU.bitwise_and)
                    dve.drain()
                    V.tensor_copy(cposf[0:R, :], cpos[0:R, :, :, :].rearrange("p a b c -> p (a b c)"))
                    dve.drain()

                def compare():
                    V.tensor_tensor(pick[0:R, :, :], cposf[0:R, :].unsqueeze(2).to_broadcast([R, 4 * TOPK, TOPK]),
                                    iota[0:R, :].unsqueeze(1).to_broadcast([R, 4 * TOPK, TOPK]), ALU.is_equal)
                    dve.drain()

                def choose():
                    q = pick[0:R, :, :].rearrange("p (m k) j -> p m k j", k=TOPK)
                    V.tensor_tensor(q, q, tif[0:R, :, :].unsqueeze(2).to_broadcast([R, 4, TOPK, TOPK]), ALU.mult)
                    dve.drain()

                def finish():
                    V.tensor_reduce(picked[0:R, :, :, :].rearrange("p a b c -> p (a b c)"), pick[0:R, :, :],
                                    AX_X, ALU.add)
                    dve.drain()
                    V.scalar_tensor_tensor(out=eidx[0:R, :, :], in0=picked[0:R, :, 0, :], scalar=float(NKEYS),
                                           in1=picked[0:R, :, 1, :], op0=ALU.mult, op1=ALU.add)
                    dve.drain()
                    V.tensor_scalar(idx[0:R, t, bass.ds(i * TOPK, 2 * TOPK)],
                                    eidx[0:R, :, :].rearrange("p a b -> p (a b)"), float(l * EXPERTS), None,
                                    ALU.add).then_inc(routed, 2)

                return [copy_scores, lambda: first8(sides), lambda: next8(sides), candidates,
                        lambda: first8(both), lambda: next8(both), positions, compare, choose, finish]

            def gather_head(l, t, i, u, vv, beside=None):
                g = head_index(l, t) + i
                into = acc2 if t == 2 else x[t]

                def reduce_u(k):
                    dve.wait_ge(u_landed[k % URING], 16 * (TOPK // URING * g + k // URING + 1))
                    nc.vector.scalar_tensor_tensor(
                        out=uring[:, k % URING, :], in0=uring[:, k % URING, :], scalar=1.0, in1=xn[t][:, :],
                        op0=ALU.mult, op1=ALU.mult, accum_out=a_raw[:, k:k + 1]).then_inc(u_used, 1)

                def weights():
                    dve.wait_ge(exp_done, g)
                    nc.vector.reciprocal(erec[:, :], esum[:, :])
                    dve.drain()
                    dve.wait_ge(gelu_done, g)
                    nc.vector.scalar_tensor_tensor(out=wgt[:, :], in0=a_gelu[:, :], scalar=erec[:, 0:1],
                                                   in1=eexp[:, :], op0=ALU.mult, op1=ALU.mult
                                                   ).then_inc(w_ready, 1)
                    dve.wait_ge(w_ready, g)

                def add_v(k):
                    n = TOPK * (g - 1) + k
                    if not (isinstance(n, int) and n == 0):
                        dve.wait_ge(v_used, n)
                    dve.wait_ge(v_landed[k % VRING], 16 * (TOPK // VRING * (g - 1) + k // VRING + 1))
                    nc.vector.scalar_tensor_tensor(
                        out=into[:, :], in0=vring[:, k % VRING, :], scalar=wgt[:, k:k + 1], in1=into[:, :],
                        op0=ALU.mult, op1=ALU.add).then_inc(v_used, 1)

                if vv:
                    dve.wait_ge(gelu_half_done, g)
                for k in range(TOPK):
                    if u:
                        reduce_u(k)
                    if vv and k == 1:
                        weights()
                        add_v(0)
                    if vv and k:
                        add_v(k)
                    for f in (beside or {}).get(k, ()):
                        f()

            def heads(l, t, first, stop, routes=None, extra=None, each=1):
                def beside(i):
                    at = {k: list(f) for k, f in (extra or {}).items()}
                    if routes:
                        for n, f in enumerate(route(*routes(i))):
                            at.setdefault(2 + n + n // 3, []).append(f)
                    return at

                if stop - first == 1:
                    gather_head(l, t, first, True, first > 0, beside(first))
                elif each == 1:
                    with dve.Fori(first, stop) as i:
                        gather_head(l, t, i, True, True, beside(i))
                else:
                    with dve.Fori(first // each, stop // each) as j:
                        for m in range(each):
                            i = j * each + m
                            gather_head(l, t, i, True, True, beside(i) if m == each - 1 else None)

            def scores_ready(l, t):
                wait_group(dve, ("s", l, t, 3))

            dve.wait_ge(x_landed, 16 * NT)
            dve.wait_ge(gain_landed, 32)
            norm_stats((0,))
            norm_apply("mix", 0, (0,))
            norm_stats((1, 2))
            norm_apply("mix", 0, (1, 2))
            did(nc.vector.memset(zeros[:, :], 0.0))
            did(nc.vector.memset(ones[:, :], 1.0))
            did(nc.vector.memset(acc2[:, :], 0.0))
            did(nc.vector.memset(wsm2[:, :, :, :], 0.0))
            dve.wait_ge(const_landed, 16 * N_CONST)
            dve.wait_ge(ws2_landed, 16 * SB)
            after(steps[0])
            for g in range(GROUPS):
                nc.vector.copy_predicated(wsm[:, g, :], tril[:, :], zeros[:, :])
                nc.vector.copy_predicated(wsm2[:, g, :, :], smask[:, :, :],
                                          ws2[:, g:g + 1, :].to_broadcast([32, SB, SS]))
            dve.drain().then_inc(ws_ready, 1)
            ln_stats((0,))
            ln_apply((0,))
            dve.wait_ge(scalar_read, G[("u", 0, KA - 1)][3])
            spatial_gate(0)
            add_groups("out", 0, (0,))
            norm_stats((0,))
            norm_apply("ffn", 0, (0,))
            scores_ready(0, 0)
            for f in route(0, 0, 0):
                f()
            dve.drain()
            dve.wait_ge(xn_ready, NORMS.index(("ffn", 0, 0)) + 1)
            heads(0, 0, 0, 1, lambda i: (0, 0, 2), {15: [lambda: ln_stats((1, 2))]})
            heads(0, 0, 1, 2, lambda i: (0, 0, 4), {0: [lambda: ln_apply((1, 2))]})
            heads(0, 0, 2, 3, lambda i: (0, 0, 6), {6: [lambda: spatial_gate(1)]})
            heads(0, 0, 3, 4, None,
                  {15: [lambda: add_groups("out", 0, (1, 2)), lambda: norm_stats((1, 2))]})
            heads(0, 0, 4, 5, None, {0: [lambda: norm_apply("ffn", 0, (1, 2))]})
            scores_ready(0, 1)
            heads(0, 0, 5, HEADS, lambda i: (0, 1, 2 * i - 10))
            gather_head(0, 0, HEADS, False, True)
            dve.wait_ge(v_used, TOPK * head_index(0, 1))
            dve.wait_ge(gain_landed, 64)
            heads(0, 1, 0, 1, lambda i: (0, 1, 6), {0: [lambda: norm_stats((0,))]})
            scores_ready(0, 2)
            heads(0, 1, 1, 2, lambda i: (0, 2, 0), {0: [lambda: norm_apply("mix", 1, (0,))]})
            heads(0, 1, 2, 3, lambda i: (0, 2, 2),
                  {0: [lambda: short_conv(2, 0)],
                   15: [lambda: add_groups("out", 1, (0,)), lambda: norm_stats((0,))]})
            heads(0, 1, 3, 4, lambda i: (0, 2, 4), {0: [lambda: norm_apply("ffn", 1, (0,))]})
            heads(0, 1, 4, 5, lambda i: (0, 2, 6))
            scores_ready(1, 0)
            heads(0, 1, 5, HEADS, lambda i: (1, 0, 2 * i - 10))

            def spread_samples(l):
                n = HEADS_OF[2] * TOPK
                dve.wait_ge(routed, route_index(l, 2) + HEADS)
                for f in range(FOLD):
                    for dst, src in ((idx2, idx), (gate2, gate)):
                        nc.vector.tensor_copy(dst[32 * f:32 * f + 32, :], src[0:32, 2, f * n:(f + 1) * n])
                dve.drain().then_inc(idx2_ready, 1)

            spread_samples(0)
            gather_head(0, 1, HEADS, False, True)
            dve.wait_ge(xn2_spread, FOLD - 1)
            heads(0, 2, 0, 1, lambda i: (1, 0, 6))
            heads(0, 2, 1, 2)
            gather_head(0, 2, HEADS_OF[2], False, True)
            dve.wait_ge(xn_ready, NORMS.index(("ffn", 1, 0)) + 1)
            heads(1, 0, 0, 1, None,
                  {1: [lambda: add_groups("fold", 0, (2,)), lambda: norm_stats((1, 2)),
                       lambda: did(nc.vector.memset(acc2[:, :], 0.0))]})
            heads(1, 0, 1, 2, None, {0: [lambda: norm_apply("mix", 1, (1, 2))]})
            heads(1, 0, 2, 3, None, {8: [lambda: short_conv(3, 1)]})
            heads(1, 0, 3, 4, None, {15: [lambda: add_groups("out", 1, (1, 2)), lambda: norm_stats((1, 2))]})
            heads(1, 0, 4, 5, None, {0: [lambda: norm_apply("ffn", 1, (1, 2))]})
            scores_ready(1, 1)
            heads(1, 0, 5, HEADS, lambda i: (1, 1, 2 * i - 10))
            gather_head(1, 0, HEADS, False, True)
            dve.wait_ge(v_used, TOPK * head_index(1, 1))
            dve.wait_ge(gain_landed, 80)
            heads(1, 1, 0, 1, lambda i: (1, 1, 6), {0: [lambda: norm_stats((0,))]})
            scores_ready(1, 2)
            heads(1, 1, 1, 2, lambda i: (1, 2, 0), {0: [lambda: norm_apply("final", 1, (0,))]})
            heads(1, 1, 2, HEADS, lambda i: (1, 2, i - 1), each=2)
            spread_samples(1)
            gather_head(1, 1, HEADS, False, True)
            dve.wait_ge(v_used, TOPK * head_index(1, 2))
            dve.wait_ge(xn2_spread, 2 * (FOLD - 1))
            heads(1, 2, 0, 1, None, {0: [lambda: norm_stats((1,))]})
            heads(1, 2, 1, 2, None, {0: [lambda: norm_apply("final", 1, (1,))]})
            gather_head(1, 2, HEADS_OF[2], False, True)
            add_groups("fold", 1, (2,))
            norm_stats((2,))
            norm_apply("final", 1, (2,))


_OUTS = {"y_tok": (TOK, D), "v_rows": (32, DA), "conv_prompt": (P, KD, 2), "conv_sample": (P, KD, SB, 2)}


def kernel(x_prompt, x_sample, state_conv, norm_mix, norm_ffn, norm_final,
           a_w_in, a_ln_g, a_ln_b, a_w_s, a_b_s, a_w_out,
           b_w_in, b_conv_w, b_w_out,
           peer_w_query, peer_sub_keys, peer_expert_u, peer_expert_v):
    import concourse.bacc as bacc
    from concourse.bass_utils import run_bass_kernel_spmd

    matrices = {"a_in": a_w_in[0], "a_out": a_w_out[0], "wq0": peer_w_query[0], "wq1": peer_w_query[1],
                "b_in": b_w_in[0], "b_out": b_w_out[0]}
    rows = np.arange(P)
    a = {
        "x_tok": np.concatenate([np.asarray(x_prompt).reshape(-1, D), np.asarray(x_sample).reshape(-1, D)]),
        "w_chunks": np.stack([np.asarray(matrices[m])[r:r + D, c:c + WCOLS].reshape(KD, P, WCOLS).transpose(1, 0, 2)
                              for m, c, r in CHUNKS]),
        "gains": np.stack([np.asarray(g) for g in
                           (norm_mix[0], norm_ffn[0], norm_mix[1], norm_ffn[1], norm_final)]),
        "ln_gain": np.asarray(a_ln_g),
        "ln_bias": np.asarray(a_ln_b),
        "w_s": np.asarray(a_w_s)[0].transpose(2, 0, 1),
        "b_s": np.asarray(a_b_s),
        "conv_w": np.asarray(b_conv_w)[0].reshape(3, KD, P).transpose(2, 0, 1),
        "conv_state": np.asarray(state_conv)[0].reshape(SB, 2, KD, P).transpose(3, 2, 0, 1),
        "sub_keys": np.asarray(peer_sub_keys).reshape(LAYERS, HP, NKEYS, P).transpose(0, 3, 1, 2),
        "expert_u": np.asarray(peer_expert_u).reshape(LAYERS * EXPERTS, D),
        "expert_v": np.asarray(peer_expert_v).reshape(LAYERS * EXPERTS, D),
        "ident_c": np.eye(P, dtype=np.float32),
        "iota_c": np.tile(np.arange(TOPK, dtype=np.float32), (P, 1)),
        "fold_c": (rows[:, None] % 32 == np.arange(32)[None, :]).astype(np.float32),
        "tril_c": (rows[:, None] > rows[None, :]).astype(np.uint32),
        "smask_c": ((np.arange(32)[:, None, None] // SS == np.arange(SB)[None, :, None])
                    & (np.arange(32)[:, None, None] % SS <= np.arange(SS)[None, None, :])).astype(np.uint32),
    }
    nc = bacc.Bacc("TRN2", target_bir_lowering=False, num_devices=1)
    arrays, aps = {}, {}
    for name, arr in a.items():
        arrays[name + "_dram"] = arr = np.ascontiguousarray(arr)
        aps[name] = nc.dram_tensor(name + "_dram", arr.shape, mybir.dt.from_np(arr.dtype), kind="ExternalInput").ap()
    for name, shape in _OUTS.items():
        aps[name] = nc.dram_tensor(name + "_dram", shape, F32, kind="ExternalOutput").ap()
    trunk(nc, **aps)
    got = run_bass_kernel_spmd(nc, [arrays], core_ids=[0]).results[0]
    y = got["y_tok_dram"]
    return (y[:256].reshape(1, 256, D), y[256:].reshape(SB, SS, D),
            got["v_rows_dram"].reshape(1, SB, SS, DA),
            got["conv_prompt_dram"].transpose(2, 1, 0).reshape(1, 1, 2, D),
            got["conv_sample_dram"].transpose(2, 3, 1, 0).reshape(1, SB, 2, D))
```
